# Optimizing a Trainium2 kernel written in Bass

```python
import math
import jax
import jax.numpy as jnp
from jax import lax
import numpy as np

D_MODEL = 1024
BATCH = 1
SEQ = 1024
DEPTH = 2
DEC_BATCH = 8
DEC_SEQ = 4
PAST_LEN = 8192
PAGE_SIZE = 128

HEAD_DIM = 64
A_HEADS = 8
A_KV_HEADS = 2
CMP_LEN = 32
CMP_STRIDE = 16
CMP_HID = 128
SEL_BLOCK = 64
N_SEL = 16
SWA_WIN = 512
B_HEADS = 4
DILATIONS = ((128, 1), (512, 4), (2048, 16))
C_HEADS = 16
C_KV_HEADS = 4
NUM_BUCKETS = 32
MAX_DISTANCE = 2048
Q_BLOCK = 128
RMS_EPS = 1e-6
NEG = -1e30
TINY = 1e-30
FORCE = 1e9

N_EVEN = (DEPTH + 1) // 2
N_ODD = DEPTH // 2
A_WIDTH = A_HEADS * HEAD_DIM
B_WIDTH = B_HEADS * HEAD_DIM
C_WIDTH = C_HEADS * HEAD_DIM
KV_A = A_KV_HEADS * HEAD_DIM
KV_C = C_KV_HEADS * HEAD_DIM
BIAS_HEADS = A_HEADS + len(DILATIONS) * B_HEADS
EVEN_SIZES = (A_WIDTH, 2 * KV_A, 2 * KV_A, 2 * KV_A, 3 * A_HEADS, A_WIDTH) + (3 * B_WIDTH,) * len(DILATIONS) + (B_WIDTH,)
ODD_SIZES = (C_WIDTH, KV_C, KV_C, C_HEADS, C_WIDTH)
EVEN_IN = sum(EVEN_SIZES)
ODD_IN = sum(ODD_SIZES)
F32 = jnp.float32

kernel_name = 'nsa_dilated_fox_hybrid_step'

def rms_norm(x, g):
    xf = x.astype(F32)
    y = xf * lax.rsqrt(jnp.mean(xf * xf, axis=-1, keepdims=True) + RMS_EPS)
    return (y * g.astype(F32)).astype(x.dtype)

def split_cols(x, sizes):
    return jnp.split(x, [int(i) for i in np.cumsum(sizes)[:-1]], axis=-1)

def t5_bucket(dist):
    n = jnp.maximum(dist, 0)
    exact = NUM_BUCKETS // 2
    ratio = jnp.log(jnp.maximum(n, 1).astype(F32) / exact) / math.log(MAX_DISTANCE / exact)
    large = jnp.minimum(exact + (ratio * (NUM_BUCKETS - exact)).astype(jnp.int32), NUM_BUCKETS - 1)
    return jnp.where(n < exact, n, large)

def masked_softmax(s, mask):
    s = jnp.where(mask, s, NEG)
    m = jnp.max(s, axis=-1, keepdims=True)
    p = jnp.where(mask, jnp.exp(s - m), 0.0)
    den = jnp.sum(p, axis=-1, keepdims=True)
    lse = (m + jnp.log(jnp.maximum(den, TINY)))[..., 0]
    return p / jnp.maximum(den, TINY), lse

def sweep_queries(fn, q, q_pos):
    B, T = q.shape[:2]
    qb = T if T <= Q_BLOCK else math.gcd(T, Q_BLOCK)
    nb = T // qb
    qs = jnp.moveaxis(q.reshape((B, nb, qb) + q.shape[2:]), 1, 0)
    outs = lax.map(lambda a: fn(a[0], a[1]), (qs, q_pos.reshape(nb, qb)))
    return tuple(jnp.moveaxis(o, 0, 1).reshape((B, T) + o.shape[3:]) for o in outs)

def gather_pages(pool, page_table):
    g = pool[page_table]
    return g.reshape((g.shape[0], g.shape[1] * g.shape[2]) + g.shape[3:])

def band_keys(k, n_prev):
    B, S = k.shape[:2]
    nb = S // Q_BLOCK
    kp = jnp.pad(k, [(0, 0), (n_prev * Q_BLOCK, 0)] + [(0, 0)] * (k.ndim - 2))
    kp = kp.reshape((B, nb + n_prev, Q_BLOCK) + k.shape[2:])
    return jnp.concatenate([kp[:, j:j + nb] for j in range(n_prev + 1)], axis=2)

def band_attention(q, k, v, max_dist, tab, dist_scale):
    B, S, H, D = q.shape
    G = k.shape[2]
    R = H // G
    nb = S // Q_BLOCK
    n_prev = -(-max_dist // Q_BLOCK)
    W = (n_prev + 1) * Q_BLOCK
    kb = band_keys(k, n_prev).astype(F32)
    vb = band_keys(v, n_prev).astype(F32)
    qb = q.reshape(B, nb, Q_BLOCK, G, R, D).astype(F32) * (D ** -0.5)
    s = jnp.einsum('bnqgrd,bnwgd->bnqgrw', qb, kb)
    i = jnp.arange(Q_BLOCK)
    m = jnp.arange(W)
    dist = n_prev * Q_BLOCK + i[:, None] - m[None, :]
    kpos = (jnp.arange(nb)[:, None] - n_prev) * Q_BLOCK + m[None, :]
    mask = ((dist >= 0) & (dist <= max_dist))[None] & (kpos >= 0)[:, None, :]
    bias = tab[t5_bucket(dist * dist_scale)].reshape(Q_BLOCK, W, G, R).transpose(0, 2, 3, 1)
    p, lse = masked_softmax(s + bias, mask[None, :, :, None, None, :])
    o = jnp.einsum('bnqgrw,bnwgd->bnqgrd', p, vb)
    return o.reshape(B, S, H, D), lse.reshape(B, S, H)

def window_sample(q, k_all, v_all, P, tab):
    B, T, H, D = q.shape
    L, G = k_all.shape[1], k_all.shape[2]
    R = H // G
    dist = P + jnp.arange(T)[:, None] - jnp.arange(L)[None, :]
    mask = (dist >= 0) & (dist < SWA_WIN)
    qg = q.reshape(B, T, G, R, D).astype(F32) * (D ** -0.5)
    s = jnp.einsum('btgrd,bsgd->btgrs', qg, k_all.astype(F32))
    bias = tab[t5_bucket(dist)].reshape(T, L, G, R).transpose(0, 2, 3, 1)
    p, _ = masked_softmax(s + bias, mask[:, None, None, :])
    return jnp.einsum('btgrs,bsgd->btgrd', p, v_all.astype(F32)).reshape(B, T, H, D)

def dilated_prompt(q, k, v, window, dil, tab):
    B, S, H, D = q.shape
    L = S // dil
    Lp = -(-L // Q_BLOCK) * Q_BLOCK

    def to_sub(x):
        x = x.reshape(B, L, dil, H, D).transpose(0, 2, 1, 3, 4).reshape(B * dil, L, H, D)
        return jnp.pad(x, ((0, 0), (0, Lp - L), (0, 0), (0, 0)))

    o, lse = band_attention(to_sub(q), to_sub(k), to_sub(v), window // dil, tab, dil)
    o = o[:, :L].reshape(B, dil, L, H, D).transpose(0, 2, 1, 3, 4).reshape(B, S, H, D)
    lse = lse[:, :L].reshape(B, dil, L, H).transpose(0, 2, 1, 3).reshape(B, S, H)
    return o, lse

def dilated_sample(q, k_all, v_all, P, window, dil, tab):
    B, T, H, D = q.shape
    j = jnp.arange(window // dil + 1)
    idx = P + jnp.arange(T)[:, None] - j[None, :] * dil
    valid = idx >= 0
    idx = jnp.maximum(idx, 0)
    kg = k_all[:, idx].astype(F32)
    vg = v_all[:, idx].astype(F32)
    s = jnp.einsum('bthd,btjhd->bthj', q.astype(F32) * (D ** -0.5), kg)
    bias = tab[t5_bucket(j * dil)].T
    p, lse = masked_softmax(s + bias, valid[:, None, :])
    return jnp.einsum('bthj,btjhd->bthd', p, vg), lse

def nsa_compress(rows, pe, w1, w2):
    B, L, G, D = rows.shape
    r = CMP_LEN // CMP_STRIDE
    n_chunk = L // CMP_STRIDE
    n_cmp = n_chunk - r + 1
    ch = rows[:, :n_chunk * CMP_STRIDE].reshape(B, n_chunk, CMP_STRIDE, G, D)
    blk = jnp.concatenate([ch[:, j:j + n_cmp] for j in range(r)], axis=2)
    blk = blk + pe[:, None, :].astype(blk.dtype)
    flat = jnp.swapaxes(blk, 2, 3).reshape(B, n_cmp, G, CMP_LEN * D)
    return jax.nn.silu(flat @ w1) @ w2

def nsa_global(q, q_pos, kc_rows, vc_rows, ks_rows, vs_rows, pe, w1, w2, tab):
    B, T, H, D = q.shape
    G = kc_rows.shape[2]
    R = H // G
    L = ks_rows.shape[1]
    kc = nsa_compress(kc_rows, pe[0], w1[0], w2[0]).astype(F32)
    vc = nsa_compress(vc_rows, pe[1], w1[1], w2[1]).astype(F32)
    n_cmp = kc.shape[1]
    cmp_end = jnp.arange(n_cmp) * CMP_STRIDE + CMP_LEN - 1
    n_slc = -(-L // SEL_BLOCK)
    n_top = min(N_SEL, n_slc)
    r_ch = SEL_BLOCK // CMP_STRIDE
    r_cmp = CMP_LEN // CMP_STRIDE

    def to_blocks(x):
        x = jnp.pad(x, ((0, 0), (0, n_slc * SEL_BLOCK - L), (0, 0), (0, 0)))
        return x.reshape(B, n_slc, SEL_BLOCK, G, D).transpose(0, 3, 1, 2, 4).astype(F32)

    ks = to_blocks(ks_rows)
    vs = to_blocks(vs_rows)
    tab_g = tab.reshape(NUM_BUCKETS, G, R)
    b_idx = jnp.arange(B)[:, None, None, None]
    g_idx = jnp.arange(G)[None, None, :, None]
    g5 = jnp.arange(G)[None, None, :, None, None]
    j_blk = jnp.arange(n_slc)

    def block_fn(qb, pos):
        Q = qb.shape[1]
        qg = qb.reshape(B, Q, G, R, D).astype(F32) * (D ** -0.5)
        dist_c = pos[:, None] - cmp_end[None, :]
        s = jnp.einsum('bqgrd,bngd->bqgrn', qg, kc)
        s = s + jnp.transpose(tab_g[t5_bucket(dist_c)], (0, 2, 3, 1))[None]
        p_cmp, _ = masked_softmax(s, (dist_c >= 0)[None, :, None, None, :])
        o_cmp = jnp.einsum('bqgrn,bngd->bqgrd', p_cmp, vc)
        pg = p_cmp.sum(axis=3)
        pg = jnp.pad(pg, ((0, 0), (0, 0), (0, 0), (r_cmp - 1, n_slc * r_ch - n_cmp)))
        chunk = sum(pg[..., j:j + n_slc * r_ch] for j in range(r_cmp))
        imp = chunk.reshape(B, Q, G, n_slc, r_ch).sum(axis=-1)
        cur = pos // SEL_BLOCK
        forced = (j_blk[None] == cur[:, None]) | (j_blk[None] == cur[:, None] - 1) | (j_blk[None] == 0)
        future = j_blk[None] > cur[:, None]
        imp = jnp.where(forced[None, :, None], FORCE, imp)
        imp = jnp.where(future[None, :, None], -1.0, imp)
        val, idx = lax.top_k(imp, n_top)
        kg = ks[b_idx, g_idx, idx]
        vg = vs[b_idx, g_idx, idx]
        kpos = idx[..., None] * SEL_BLOCK + jnp.arange(SEL_BLOCK)
        dist_s = pos[None, :, None, None, None] - kpos
        mask = (val >= 0)[..., None] & (dist_s >= 0)
        s2 = jnp.einsum('bqgrd,bqgksd->bqgrks', qg, kg)
        s2 = s2 + jnp.moveaxis(tab_g[t5_bucket(dist_s), g5], -1, 3)
        s2 = s2.reshape(B, Q, G, R, n_top * SEL_BLOCK)
        p_sel, _ = masked_softmax(s2, mask.reshape(B, Q, G, 1, n_top * SEL_BLOCK))
        o_sel = jnp.einsum('bqgrm,bqgmd->bqgrd', p_sel, vg.reshape(B, Q, G, n_top * SEL_BLOCK, D))
        return o_cmp.reshape(B, Q, H, D), o_sel.reshape(B, Q, H, D)

    return sweep_queries(block_fn, q, q_pos)

def fox_attention(q, q_pos, k, v, logf):
    B, T, H, D = q.shape
    L, G = k.shape[1], k.shape[2]
    R = H // G
    c = jnp.cumsum(logf.astype(F32), axis=1)
    c_k = c.reshape(B, L, G, R).transpose(0, 2, 3, 1)
    kf, vf = k.astype(F32), v.astype(F32)
    kpos = jnp.arange(L)

    def block_fn(qb, pos):
        Q = qb.shape[1]
        qg = qb.reshape(B, Q, G, R, D).astype(F32) * (D ** -0.5)
        c_q = c[:, pos].reshape(B, Q, G, R, 1)
        s = jnp.einsum('bqgrd,blgd->bqgrl', qg, kf) + (c_q - c_k[:, None])
        p, _ = masked_softmax(s, (kpos[None, :] <= pos[:, None])[None, :, None, None, :])
        return (jnp.einsum('bqgrl,blgd->bqgrd', p, vf).reshape(B, Q, H, D),)

    (o,) = sweep_queries(block_fn, q, q_pos)
    return o

def even_layer(x, norm_g, w_in, w_out, cmp_pe, cmp_w1, cmp_w2, tab, past):
    B, T, _ = x.shape
    past_len = 0 if past is None else past[0].shape[1]
    q_pos = past_len + jnp.arange(T, dtype=jnp.int32)
    parts = split_cols(rms_norm(x, norm_g) @ w_in, EVEN_SIZES)
    q_a, kv_cmp, kv_sel, kv_win, g_a, z_a = parts[:6]
    z_b = parts[-1]
    G = A_KV_HEADS
    q_a = q_a.reshape(B, T, A_HEADS, HEAD_DIM)
    nsa_new = jnp.concatenate([kv_cmp.reshape(B, T, 2, G, HEAD_DIM), kv_sel.reshape(B, T, 2, G, HEAD_DIM)], axis=2)
    win_new = kv_win.reshape(B, T, 2, G, HEAD_DIM)
    tab_a = tab[:, :A_HEADS]
    if past is None:
        nsa_all = nsa_new
        o_win, _ = band_attention(q_a, win_new[:, :, 0], win_new[:, :, 1], SWA_WIN - 1, tab_a, 1)
        win_state = win_new[:, T - min(SWA_WIN, T):]
    else:
        nsa_past, win_buf, dil_bufs = past
        nsa_all = jnp.concatenate([nsa_past, nsa_new], axis=1)
        win_all = jnp.concatenate([win_buf, win_new], axis=1)
        o_win = window_sample(q_a, win_all[:, :, 0], win_all[:, :, 1], win_buf.shape[1], tab_a)
        win_state = win_all[:, T:]
    o_cmp, o_sel = nsa_global(q_a, q_pos, nsa_all[:, :, 0], nsa_all[:, :, 1], nsa_all[:, :, 2], nsa_all[:, :, 3],
                              cmp_pe, cmp_w1, cmp_w2, tab_a)
    gate = jax.nn.sigmoid(g_a.astype(F32)).reshape(B, T, 3, A_HEADS, 1)
    o_a = gate[:, :, 0] * o_cmp + gate[:, :, 1] * o_sel + gate[:, :, 2] * o_win
    outs, lses, dil_states = [], [], []
    for gi, (window, dil) in enumerate(DILATIONS):
        q, k, v = (t.reshape(B, T, B_HEADS, HEAD_DIM) for t in split_cols(parts[6 + gi], (B_WIDTH,) * 3))
        tab_g = tab[:, A_HEADS + gi * B_HEADS:A_HEADS + (gi + 1) * B_HEADS]
        kv_new = jnp.stack([k, v], axis=2)
        if past is None:
            o, lse = dilated_prompt(q, k, v, window, dil, tab_g)
            dil_states.append(kv_new[:, T - min(window, T):])
        else:
            kv_all = jnp.concatenate([dil_bufs[gi], kv_new], axis=1)
            o, lse = dilated_sample(q, kv_all[:, :, 0], kv_all[:, :, 1], dil_bufs[gi].shape[1], window, dil, tab_g)
            dil_states.append(kv_all[:, T:])
        outs.append(o)
        lses.append(lse)
    wts = jax.nn.softmax(jnp.stack(lses), axis=0)[..., None]
    o_b = jnp.sum(wts * jnp.stack(outs), axis=0)
    mix = jnp.concatenate([o_a.reshape(B, T, A_WIDTH) * jax.nn.silu(z_a.astype(F32)),
                           o_b.reshape(B, T, B_WIDTH) * jax.nn.silu(z_b.astype(F32))], axis=-1)
    y = x + mix.astype(x.dtype) @ w_out
    return y, (nsa_new, win_state, tuple(dil_states))

def odd_layer(x, norm_g, w_in, b_f, w_out, past):
    B, T, _ = x.shape
    past_len = 0 if past is None else past[0].shape[1]
    q_pos = past_len + jnp.arange(T, dtype=jnp.int32)
    q, k, v, f, z = split_cols(rms_norm(x, norm_g) @ w_in, ODD_SIZES)
    q = q.reshape(B, T, C_HEADS, HEAD_DIM)
    kv_new = jnp.stack([k.reshape(B, T, C_KV_HEADS, HEAD_DIM), v.reshape(B, T, C_KV_HEADS, HEAD_DIM)], axis=2)
    logf = jax.nn.log_sigmoid(f.astype(F32) + b_f.astype(F32))
    if past is None:
        kv_all, lf_all = kv_new, logf
    else:
        kv_all = jnp.concatenate([past[0], kv_new], axis=1)
        lf_all = jnp.concatenate([past[1].astype(F32), logf], axis=1)
    o = fox_attention(q, q_pos, kv_all[:, :, 0], kv_all[:, :, 1], lf_all)
    mix = o.reshape(B, T, C_WIDTH) * jax.nn.silu(z.astype(F32))
    return x + mix.astype(x.dtype) @ w_out, (kv_new, logf)

def setup_inputs(seed: int = 0) -> dict:
    key = jax.random.key(seed)
    keys = iter(jax.random.split(key, 32))
    n_pages = PAST_LEN // PAGE_SIZE
    n_pool = (5 * DEC_BATCH * n_pages + 3) // 4

    def nrm(shape, scale=1.0):
        return scale * jax.random.normal(next(keys), shape, F32)

    page_table = jax.random.permutation(next(keys), n_pool)[:DEC_BATCH * n_pages].reshape(DEC_BATCH, n_pages).astype(jnp.int32)
    return {
        'x_prompt': nrm((BATCH, SEQ, D_MODEL)),
        'x_sample': nrm((DEC_BATCH, DEC_SEQ, D_MODEL)),
        'cache_nsa': nrm((N_EVEN, n_pool, PAGE_SIZE, 4, A_KV_HEADS, HEAD_DIM)),
        'cache_nsa_win': nrm((N_EVEN, DEC_BATCH, min(SWA_WIN, PAST_LEN), 2, A_KV_HEADS, HEAD_DIM)),
        'cache_dil_w128': nrm((N_EVEN, DEC_BATCH, min(DILATIONS[0][0], PAST_LEN), 2, B_HEADS, HEAD_DIM)),
        'cache_dil_w512': nrm((N_EVEN, DEC_BATCH, min(DILATIONS[1][0], PAST_LEN), 2, B_HEADS, HEAD_DIM)),
        'cache_dil_w2048': nrm((N_EVEN, DEC_BATCH, min(DILATIONS[2][0], PAST_LEN), 2, B_HEADS, HEAD_DIM)),
        'cache_fox': nrm((N_ODD, n_pool, PAGE_SIZE, 2, C_KV_HEADS, HEAD_DIM)),
        'cache_fox_logf': jax.nn.log_sigmoid(2.0 + nrm((N_ODD, n_pool, PAGE_SIZE, C_HEADS))),
        'page_table': page_table,
        'rel_bias': nrm((NUM_BUCKETS, BIAS_HEADS), 0.5),
        'norm_e': 1.0 + nrm((N_EVEN, D_MODEL), 0.05),
        'w_in_e': nrm((N_EVEN, D_MODEL, EVEN_IN), D_MODEL ** -0.5),
        'cmp_pe': nrm((N_EVEN, 2, CMP_LEN, HEAD_DIM), 0.1),
        'cmp_w1': nrm((N_EVEN, 2, CMP_LEN * HEAD_DIM, CMP_HID), (CMP_LEN * HEAD_DIM) ** -0.5),
        'cmp_w2': nrm((N_EVEN, 2, CMP_HID, HEAD_DIM), CMP_HID ** -0.5),
        'w_out_e': nrm((N_EVEN, A_WIDTH + B_WIDTH, D_MODEL), (A_WIDTH + B_WIDTH) ** -0.5),
        'norm_o': 1.0 + nrm((N_ODD, D_MODEL), 0.05),
        'w_in_o': nrm((N_ODD, D_MODEL, ODD_IN), D_MODEL ** -0.5),
        'b_f': 2.0 + nrm((N_ODD, C_HEADS), 0.1),
        'w_out_o': nrm((N_ODD, C_WIDTH, D_MODEL), C_WIDTH ** -0.5),
        'norm_f': 1.0 + nrm((D_MODEL,), 0.05),
    }

def reference(x_prompt, x_sample, cache_nsa, cache_nsa_win, cache_dil_w128, cache_dil_w512, cache_dil_w2048,
              cache_fox, cache_fox_logf, page_table, rel_bias, norm_e, w_in_e, cmp_pe, cmp_w1, cmp_w2, w_out_e,
              norm_o, w_in_o, b_f, w_out_o, norm_f):
    dil_caches = (cache_dil_w128, cache_dil_w512, cache_dil_w2048)
    hp, hs = x_prompt, x_sample
    nsa_p, nsa_s, win_p, win_s = [], [], [], []
    fox_p, fox_s, lf_p, lf_s = [], [], [], []
    dil_p = [[] for _ in DILATIONS]
    dil_s = [[] for _ in DILATIONS]
    for layer in range(DEPTH):
        li = layer // 2
        if layer % 2 == 0:
            wts = (norm_e[li], w_in_e[li], w_out_e[li], cmp_pe[li], cmp_w1[li], cmp_w2[li], rel_bias)
            hp, (nsa_new, win_new, dil_new) = even_layer(hp, *wts, None)
            past = (gather_pages(cache_nsa[li], page_table), cache_nsa_win[li], tuple(c[li] for c in dil_caches))
            hs, (nsa_new_s, win_new_s, dil_new_s) = even_layer(hs, *wts, past)
            nsa_p.append(nsa_new)
            nsa_s.append(nsa_new_s)
            win_p.append(win_new)
            win_s.append(win_new_s)
            for gi in range(len(DILATIONS)):
                dil_p[gi].append(dil_new[gi])
                dil_s[gi].append(dil_new_s[gi])
        else:
            wts = (norm_o[li], w_in_o[li], b_f[li], w_out_o[li])
            hp, (kv_new, lf_new) = odd_layer(hp, *wts, None)
            past = (gather_pages(cache_fox[li], page_table), gather_pages(cache_fox_logf[li], page_table))
            hs, (kv_new_s, lf_new_s) = odd_layer(hs, *wts, past)
            fox_p.append(kv_new)
            fox_s.append(kv_new_s)
            lf_p.append(lf_new)
            lf_s.append(lf_new_s)
    y_prompt = rms_norm(hp, norm_f)
    y_sample = rms_norm(hs, norm_f)
    new_nsa_prompt = jnp.stack(nsa_p)
    new_nsa_sample = jnp.stack(nsa_s)
    new_win_prompt = jnp.stack(win_p)
    new_win_sample = jnp.stack(win_s)
    new_dil128_prompt = jnp.stack(dil_p[0])
    new_dil128_sample = jnp.stack(dil_s[0])
    new_dil512_prompt = jnp.stack(dil_p[1])
    new_dil512_sample = jnp.stack(dil_s[1])
    new_dil2048_prompt = jnp.stack(dil_p[2])
    new_dil2048_sample = jnp.stack(dil_s[2])
    new_fox_prompt = jnp.stack(fox_p)
    new_fox_sample = jnp.stack(fox_s)
    new_logf_prompt = jnp.stack(lf_p)
    new_logf_sample = jnp.stack(lf_s)
    return (y_prompt, y_sample, new_nsa_prompt, new_nsa_sample, new_win_prompt, new_win_sample,
            new_dil128_prompt, new_dil128_sample, new_dil512_prompt, new_dil512_sample,
            new_dil2048_prompt, new_dil2048_sample, new_fox_prompt, new_fox_sample,
            new_logf_prompt, new_logf_sample)


_drawn_inputs = setup_inputs


def setup_inputs(seed=0):
    import zlib

    import numpy as np

    out = dict(_drawn_inputs(seed))
    spreads = {}
    factors = {'cache_nsa': 3.221, 'cmp_pe': 4.245}
    for name, (base, spread) in spreads.items():
        noise = np.random.default_rng([zlib.crc32(name.encode()), seed]).standard_normal(out[name].shape)
        drawn = base * np.exp(spread * noise) if base else spread * noise
        out[name] = jnp.asarray(drawn.astype(out[name].dtype))
    for name, factor in factors.items():
        out[name] = (out[name] * factor).astype(out[name].dtype)
    return out
```

```python
import math
from contextlib import ExitStack, contextmanager

import numpy as np
import concourse.bass as bass
from concourse import mybir

F32 = mybir.dt.float32
ALU = mybir.AluOpType
ACT = mybir.ActivationFunctionType
AX = mybir.AxisListType
ds = bass.ds

D_MODEL = 1024
SEQ = 1024
DEC_BATCH = 8
DEC_SEQ = 4
PAST = 8192
PAGE = 128
HD = 64
A_HEADS, A_KV, B_HEADS, C_HEADS, C_KV = 8, 2, 4, 16, 4
WIN = 512
DILATIONS = ((128, 1), (512, 4), (2048, 16))
N_SEL, SEL_BLOCK = 16, 64
CMP_LEN, CMP_STRIDE, CMP_HID = 32, 16, 128
NUM_BUCKETS, MAX_DISTANCE = 32, 2048
EPS = 1e-6
NEG = -1e30
FORCE = 1e9
TINY = 1e-30
N_TOK = DEC_BATCH * DEC_SEQ
N_ALL = SEQ + N_TOK
TILES = SEQ // 128
BIAS_HEADS = A_HEADS + 3 * B_HEADS
N_PAGES = PAST // PAGE
N_POOL = (5 * DEC_BATCH * N_PAGES + 3) // 4
SCALE = HD ** -0.5

QA, KCMP, VCMP, KSEL, VSEL, KWIN, VWIN, GA, ZA, B0 = 0, 512, 640, 768, 896, 1024, 1152, 1280, 1304, 1816
ZB = B0 + 3 * 768
EVEN_IN = ZB + 256
QC, KC, VC, FC, ZC = 0, 1024, 1280, 1536, 1552
ODD_IN = ZC + 1024
OW = HD + 2

CMP_OUT = [(8 * N_PAGES - 1), (SEQ // CMP_STRIDE - 1)]


def bucket(dist):
    n = np.maximum(dist, 0)
    exact = NUM_BUCKETS // 2
    ratio = np.log(np.maximum(n, 1).astype(np.float32) / np.float32(exact)) / np.float32(math.log(MAX_DISTANCE / exact))
    large = np.minimum(exact + (ratio * np.float32(NUM_BUCKETS - exact)).astype(np.int32), NUM_BUCKETS - 1)
    return np.where(n < exact, n, large)


def one_hot(dist, valid):
    b = np.where(valid, bucket(dist), NUM_BUCKETS)
    return (b[None] == np.arange(NUM_BUCKETS + 1).reshape((-1,) + (1,) * b.ndim)).astype(np.float32)


def constants():
    c = {}
    c["ident"] = np.eye(128, dtype=np.float32)
    c["flip"] = np.ascontiguousarray(np.eye(128, dtype=np.float32)[::-1])
    i = np.arange(128)
    c["causal"] = np.where(i[:, None] >= i[None], 0, NEG).astype(np.float32)
    c["same_half"] = np.where(i[:, None] // 64 == i[None] // 64, 0, NEG).astype(np.float32)
    c["upto"] = (i[:, None] <= i[None]).astype(np.float32)
    c["after"] = (i[:, None] > i[None]).astype(np.float32)
    d = 1023 - np.arange(1152)
    c["oh_rows"] = np.stack([one_hot(d, (d >= 0) & ok) for ok in
                             (d < WIN, d >= 0, d <= 128)] +
                            [one_hot(d * dil, (d >= 0) & (d <= w // dil)) for w, dil in DILATIONS[1:]], 1).astype(np.float32)
    u = np.arange(120)
    d = i[None] - 16 * (u[:, None] - 56) - 31
    c["oh_cmp_p"] = one_hot(d, d >= 0)
    t = np.arange(4)[None, :, None]
    key = i[None, None, :]
    new_d = t - key
    new = (key <= t) & (key < 4)

    def tiles(dist, valid, nd=new_d, nv=new):
        return one_hot(np.concatenate([nd, dist], 0), np.concatenate([nv, valid], 0))

    n = np.arange(4)[:, None, None]
    d = 512 + t - (128 * n + key)
    c["oh_win"] = tiles(d, d < WIN)
    d = PAST + t - (128 * np.arange(N_PAGES)[:, None, None] + key)
    c["oh_sel"] = tiles(d, d >= 0)
    d = 128 + t - key
    c["oh_b0"] = tiles(d, d <= 128)
    for g, (w, dil) in enumerate(DILATIONS[1:], 1):
        d = w - dil * key + 0 * n + 0 * t
        c[f"oh_b{g}"] = tiles(d, (n == t) & (key >= 0), 0 * new_d, (key == t))
    d = PAST + t - (16 * (128 * n + key) + CMP_LEN - 1)
    c["oh_cmp"] = one_hot(d, (d >= 0) & (128 * n + key < CMP_OUT[0]))
    ncmp = np.arange(512)
    w = np.zeros((512, 129), np.float32)
    for k in range(CMP_OUT[0]):
        for ch in (k, k + 1):
            w[k, ch // 4] += 1
    c["blocks"] = np.ascontiguousarray(w.reshape(4, 128, 129).transpose(1, 0, 2))
    forced = np.zeros((1, 129), np.float32)
    forced[0, [0, 127, 128]] = 1
    c["forced"] = np.repeat(np.concatenate([1 - forced, forced * FORCE], 0)[None], 8, 0)
    c["halves"] = (np.arange(2)[:, None] == i[None] // 64).astype(np.float32)
    t = np.arange(N_TOK)
    c["seq_upto"] = ((t[:, None] <= t[None]) & (t[:, None] // 4 == t[None] // 4)).astype(np.float32)
    c["new_mask"] = np.where(t[:, None] % 4 <= np.arange(4)[None], 0, NEG).astype(np.float32)
    rows = []
    for r in (4, 1):
        x = (np.arange(64) // (4 * r)) % 2
        rows += [1 - x, x]
    c["half_of"] = np.stack(rows, 1).astype(np.float32)
    return c


class Env:
    pass


@contextmanager
def signals(nc, name):
    held = []

    def sem(n):
        held.append(nc.alloc_semaphore(f"{name}_{n}"))
        return held[-1]
    yield sem
    nc.clear_and_free_semaphores(held)
    nc.all_engine_barrier()


def shift_states(eng, E, b):
    for src, dst in ((E.cache_nsa_win, E.o_win_sample), (E.cache_dil_w128, E.o_dil0_sample), (E.cache_dil_w512, E.o_dil1_sample),
                     (E.cache_dil_w2048, E.o_dil2_sample)):
        v = [x[0].rearrange("b t x g d -> b t (x g d)") for x in (src, dst)]
        T = v[0].shape[1]
        eng.dma_start(v[1][b, 0:T - DEC_SEQ, :], v[0][b, DEC_SEQ:T, :]).then_inc(E.states, 16)


def project(nc, E, name, sources, gain, weights, out, width, chunks, tail, with_chunk=None):
    KT = D_MODEL // 128
    with ExitStack() as s:
        sb = lambda n, sh: s.enter_context(nc.sbuf_tensor(f"{name}_{n}", sh, F32))
        sem = s.enter_context(signals(nc, name))
        PS = E.PS
        xT = sb("xT", [128, KT, N_ALL])
        x = sb("x", [128, D_MODEL])
        xn = sb("xn", [128, D_MODEL])
        sq = sb("sq", [128, D_MODEL])
        g = sb("g", [128, D_MODEL])
        st = sb("st", [128, 4])
        w = sb("w", [128, 2, KT, 512])
        o = sb("o", [128, TILES + 1, 512])
        x_in, x_free, sumsq, mean, root, normed, turned, xt_done = map(sem, (
            "x_in", "x_free", "sumsq", "mean", "root", "normed", "turned", "xt_done"))
        w_free, prod, evac, g_in, junk = map(sem, ("w_free", "prod", "evac", "g_in", "junk"))
        w_in = [sem("w_in0"), sem("w_in1")]
        stored = [sem(f"stored{t}") for t in range(TILES + 1)]
        with nc.Block() as block:
            def tiles(eng, body):
                with eng.Fori(0, TILES) as i:
                    body(i, 128)
                body(TILES, N_TOK)

            @block.sync
            def _(sp):
                sp.dma_start(g[:], gain.to_broadcast([128, D_MODEL])).then_inc(g_in, 16)

                def body(i, n):
                    sp.wait_ge(x_free, i + 1)
                    sp.dma_start(x[0:n, :], sources(i, n)).then_inc(x_in, 16)
                tiles(sp, body)

            @block.scalar
            def _(act):
                def body(i, n):
                    act.wait_ge(x_in, 16 * i + 16)
                    nc.scalar.activation(sq[0:n, :], x[0:n, :], ACT.Square, accum_out=st[0:n, 0:1]).then_inc(sumsq, 1)
                    act.wait_ge(mean, i + 1)
                    nc.scalar.activation(st[0:n, 2:3], st[0:n, 1:2], ACT.Sqrt).then_inc(root, 1)
                tiles(act, body)

            @block.vector
            def _(dve):
                dve.sem_inc(x_free, 1)
                dve.wait_ge(g_in, 16)

                def body(i, n):
                    dve.wait_ge(sumsq, i + 1)
                    nc.vector.tensor_scalar(st[0:n, 1:2], st[0:n, 0:1], 1.0 / D_MODEL, EPS, ALU.mult, ALU.add).then_inc(mean, 1)
                    dve.wait_ge(root, i + 1)
                    nc.vector.reciprocal(st[0:n, 3:4], st[0:n, 2:3])
                    dve.drain()
                    nc.vector.scalar_tensor_tensor(xn[0:n, :], x[0:n, :], st[0:n, 3:4], g[0:n, :], ALU.mult, ALU.mult).then_inc(normed, 1)
                    dve.drain().then_inc(x_free, 1)
                    dve.wait_ge(turned, i + 1)
                    nc.vector.tensor_copy(xT[:, :, ds(i * 128, n)],
                                          PS[:, 0:8 * n].rearrange("p (k t) -> p k t", k=KT)).then_inc(xt_done, 1)
                tiles(dve, body)

            @block.tensor
            def _(pe):
                def body(i, n):
                    pe.wait_ge(normed, i + 1)
                    pe.sem_inc(junk, 1)
                    for k in range(KT):
                        last = nc.tensor.transpose(PS[:, k * n:(k + 1) * n], xn[0:n, k * 128:(k + 1) * 128], E.ident[0:n, 0:n])
                    last.then_inc(turned, 1)
                tiles(pe, body)
        with nc.Block() as block:
            def all_chunks(eng, body):
                with eng.Fori(0, chunks // 2) as c2:
                    body(c2 * 2, c2, 0, width)
                    body(c2 * 2 + 1, c2, 1, width)
                if chunks % 2:
                    body(chunks - 1, chunks // 2, 0, width)
                if tail:
                    body(chunks, chunks // 2, chunks % 2, tail)

            def size(t):
                return 128 if t < TILES else N_TOK

            @block.sync
            def _(sp):
                def body(c, c2, half, n):
                    sp.wait_ge(w_free, c + 1)
                    sp.dma_start(w[:, half, :, 0:n],
                                 weights[:, ds(c * width, n)].rearrange("(k p) n -> p k n", p=128)).then_inc(w_in[half], 16)
                    if with_chunk and n == width:
                        with_chunk(sp, E, c)
                all_chunks(sp, body)

            @block.tensor
            def _(pe):
                pe.sem_inc(w_free, 2)

                def body(c, c2, half, n):
                    for t in range(TILES + 1):
                        if t == 0:
                            pe.wait_ge(w_in[half], c2 * 16 + 16)
                            pe.sem_inc(junk, 1)
                        pe.wait_ge(evac, c * (TILES + 1) + t + 1)
                        pe.sem_inc(junk, 1)
                        bank = (half * (TILES + 1) + t) % 6
                        for k in range(KT):
                            last = nc.tensor.matmul(PS[0:size(t), bank * 512:bank * 512 + n],
                                                    xT[:, k, t * 128:t * 128 + size(t)], w[:, half, k, 0:n],
                                                    start=(k == 0), stop=(k == KT - 1))
                        last.then_inc(prod, 1)
                    pe.drain().then_inc(w_free, 1)
                all_chunks(pe, body)

            @block.vector
            def _(dve):
                dve.sem_inc(evac, 6)

                def body(c, c2, half, n):
                    for t in range(TILES + 1):
                        dve.wait_ge(prod, c * (TILES + 1) + t + 1)
                        dve.sem_inc(junk, 1)
                        dve.wait_ge(stored[t], c * 16 + 16)
                        bank = (half * (TILES + 1) + t) % 6
                        nc.vector.tensor_copy(o[0:size(t), t, 0:n], PS[0:size(t), bank * 512:bank * 512 + n]).then_inc(evac, 1)
                all_chunks(dve, body)

            @block.scalar
            def _(act):
                for t in range(TILES + 1):
                    act.sem_inc(stored[t], 16)

                def body(c, c2, half, n):
                    for t in range(TILES + 1):
                        act.wait_ge(evac, c * (TILES + 1) + t + 7)
                        act.dma_start(out[t * 128:t * 128 + size(t), ds(c * width, n)], o[0:size(t), t, 0:n]).then_inc(stored[t], 16)
                all_chunks(act, body)
                for t in range(TILES + 1):
                    act.wait_ge(stored[t], 16 * (chunks + bool(tail)) + 16)


def make_bias_rows(nc, E):
    kinds = [(0, 0, 8), (1, 0, 8), (2, 8, 4), (3, 12, 4), (4, 16, 4)]
    n = 1152
    with ExitStack() as s:
        sb = lambda nm, sh: s.enter_context(nc.sbuf_tensor(f"rows_{nm}", sh, F32))
        oh = sb("oh", [33, 5, n])
        ohc = sb("ohc", [33, 120, 128])
        r = sb("r", [8, 5, n])
        cmp_b = sb("cmp", [128, 8, 120])
        sem = s.enter_context(signals(nc, "rows"))
        loaded, prod, copied, stored = map(sem, ("loaded", "prod", "copied", "stored"))
        cuts = [(0, 512), (512, 1024), (1024, n)]
        with nc.Block() as block:
            @block.sync
            def _(sp):
                sp.dma_start(oh[:], E.c_oh_rows).then_inc(loaded, 16)
                sp.dma_start(ohc[:], E.c_oh_cmp_p).then_inc(loaded, 16)
                sp.wait_ge(copied, 17)
                at = 0
                for k, h0, nh in kinds:
                    sp.dma_start(E.rows[at:at + nh, :], r[0:nh, k, :]).then_inc(stored, 16)
                    at += nh
                sp.dma_start(E.cmp_rows.rearrange("h p u -> p h u"), cmp_b[:]).then_inc(stored, 16)
                sp.wait_ge(stored, 96)

            @block.tensor
            def _(pe):
                pe.wait_ge(loaded, 32)
                for k, h0, nh in kinds:
                    if k:
                        pe.wait_ge(copied, 3 * k)
                    for a, b in cuts:
                        nc.tensor.matmul(E.PS[0:nh, a:b], E.tabx[:, h0:h0 + nh], oh[:, k, a:b], start=True, stop=True).then_inc(prod, 1)
                for u in range(120):
                    o = 1536 + 512 * (u // 60) + 8 * (u % 60)
                    last = nc.tensor.matmul(E.PS[:, o:o + 8], ohc[:, u, :], E.tabx[:, 0:8], start=True, stop=True)
                last.then_inc(prod, 1)

            @block.vector
            def _(dve):
                for k, h0, nh in kinds:
                    for j, (a, b) in enumerate(cuts):
                        dve.wait_ge(prod, 3 * k + j + 1)
                        nc.vector.tensor_copy(r[0:nh, k, a:b], E.PS[0:nh, a:b]).then_inc(copied, 1)
                dve.wait_ge(prod, 16)
                for j in range(2):
                    nc.vector.tensor_copy(cmp_b[:, :, 60 * j:60 * j + 60],
                                          E.PS[:, 1536 + 512 * j:1536 + 512 * j + 480].rearrange("p (u h) -> p h u", h=8)).then_inc(copied, 1)


def prompt_attention(nc, E, name, kv_heads, R, src, q0, k0, v0, out, bias, first_key, order=1):
    H = kv_heads * R
    cmp = bias[0] == "cmp"
    fox = bias[0] == "fox"
    KW = CMP_OUT[1] if cmp else 128
    first = (lambda n: n) if cmp else first_key
    count = [n - first(n) + 1 for n in range(TILES)]
    groups = [-(-c // 4) for c in count]
    NG = sum(groups)
    g_before = [sum(groups[:n]) for n in range(TILES + 1)]
    preps = 3 if cmp else 4
    flips = 0 if cmp or fox else (1 if bias[0] == "halves" else 2)
    NP = preps + flips
    with ExitStack() as s:
        sb = lambda n, sh: s.enter_context(nc.sbuf_tensor(f"{name}_{n}", sh, F32))
        sem = s.enter_context(signals(nc, name))
        PS = E.PS
        qn, kn, vn = sb("qn", [128, TILES, HD]), sb("kn", [128, TILES, HD]), sb("vn", [128, TILES, HD])
        qT, kT = sb("qT", [HD, SEQ]), sb("kT", [HD, SEQ])
        vs = sb("vs", [128, TILES, HD])
        raw = sb("raw", [128, 1024])
        tb = sb("tb", [128, 1024])
        cq = sb("cq", [128, TILES])
        S = sb("S", [128, 2, 1024])
        pT = sb("pT", [128, 2, 1024])
        st = sb("st", [128, TILES, 4])
        o = sb("o", [128, TILES, OW])
        (q_in, k_in, v_in, b_in, q_free, v_free, b_free, prep_done, prep_copied, v_copied, b_copied, score, s_free, limit, prob,
         turned, turned_copied, value, out_done, out_stored, o_free, junk) = map(sem, (
             "q_in", "k_in", "v_in", "b_in", "q_free", "v_free", "b_free", "prep_done", "prep_copied", "v_copied", "b_copied",
             "score", "s_free", "limit", "prob", "turned", "turned_copied", "value", "out_done", "out_stored", "o_free", "junk"))
        n_dma = {1: 1, 4: 4, 16: 2}[order]

        def dilated(ap, tile, load, eng, signal):
            if order == 1:
                pairs = [(ap[0:SEQ].rearrange("(n p) c -> p n c", p=128), tile)]
            elif order == 4:
                v = ap[0:SEQ].rearrange("(a p r) c -> r p a c", r=4, p=128)
                pairs = [(v[r], tile[:, 2 * r:2 * r + 2, :]) for r in range(4)]
            else:
                v = ap[0:SEQ].rearrange("(m n s) c -> s m n c", s=2, n=8)
                pairs = [(v[r], tile[64 * r:64 * r + 64, :, :]) for r in range(2)]
            for d, t in pairs:
                (eng.dma_start(t, d) if load else eng.dma_start(d, t)).then_inc(signal, 16)

        def s_at(n, a, b):
            return PS[:, (n % 2) * 1024 + a:(n % 2) * 1024 + b]

        def t_at(i, a, b):
            return PS[0:KW, 2048 + (i % 2) * 512 + a:2048 + (i % 2) * 512 + b]

        with nc.Block() as block:
            @block.sync
            def _(sp):
                with sp.Fori(0, kv_heads) as g:
                    with sp.Fori(0, R) as r:
                        h = g * R + r
                        sp.wait_ge(q_free, h + 1)
                        dilated(src[:, ds(q0 + h * HD, HD)], qn[:], True, sp, q_in)
                        if cmp:
                            sp.dma_start(kn[0:KW, 0, :], E.kc_p[0:KW, ds(g * HD, HD)]).then_inc(k_in, 16)
                        else:
                            dilated(src[:, ds(k0 + g * HD, HD)], kn[:], True, sp, k_in)
                        sp.wait_ge(v_free, h + 1)
                        if cmp:
                            sp.dma_start(vn[0:KW, 0, :], E.vc_p[0:KW, ds(g * HD, HD)]).then_inc(v_in, 16)
                        else:
                            dilated(src[:, ds(v0 + g * HD, HD)], vn[:], True, sp, v_in)
                        sp.wait_ge(b_free, h + 1)
                        if cmp:
                            sp.dma_start(raw[:, 0:120], E.cmp_rows[h]).then_inc(b_in, 16)
                        elif fox:
                            sp.dma_start(raw[:], E.neg_c[ds(h, 1), :].to_broadcast([128, SEQ])).then_inc(b_in, 16)
                        else:
                            v = E.rows[ds(bias[1] + h, 1), 0:1024]
                            v = bass.AP(v.tensor, v.offset, [[1, 128], [1, 1024]])
                            sp.dma_start(raw[:], v).then_inc(b_in, 16)

            @block.gpsimd
            def _(pool):
                pool.sem_inc(v_free, 1)
                pool.sem_inc(b_free, 1)
                pool.sem_inc(o_free, 1)
                with pool.Fori(0, H) as h:
                    pool.wait_ge(v_in, 16 * (1 if cmp else n_dma) * (h + 1))
                    pool.sem_inc(junk, 1)
                    pool.wait_ge(value, TILES * h + 1)
                    pool.sem_inc(junk, 1)
                    if cmp:
                        nc.gpsimd.tensor_copy(vs[0:KW, 0, :], vn[0:KW, 0, :]).then_inc(v_copied, 1)
                    else:
                        nc.gpsimd.tensor_copy(vs[:], vn[:]).then_inc(v_copied, 1)
                    pool.wait_ge(v_copied, h + 1)
                    pool.sem_inc(v_free, 1)
                    if cmp or fox:
                        pool.wait_ge(b_in, 16 * (h + 1))
                        pool.sem_inc(junk, 1)
                        pool.wait_ge(s_free, TILES * h + 2)
                        pool.sem_inc(junk, 1)
                        if cmp:
                            nc.gpsimd.tensor_copy(tb[:, 0:120], raw[:, 0:120]).then_inc(b_copied, 1)
                        else:
                            nc.gpsimd.tensor_copy(tb[:], raw[:]).then_inc(b_copied, 1)
                        pool.wait_ge(b_copied, h + 1)
                        pool.sem_inc(b_free, 1)
                    pool.wait_ge(out_done, TILES * (h + 1) + 1)
                    pool.sem_inc(junk, 1)
                    dilated(out[:, ds(h * OW, OW)], o[:], False, pool, out_stored)
                    pool.wait_ge(out_stored, 16 * n_dma * (h + 1))
                    pool.sem_inc(o_free, 1)

            @block.tensor
            def _(pe):
                pe.sem_inc(value, 1)
                pe.sem_inc(q_free, 1)
                with pe.Fori(0, H) as h:
                    pe.wait_ge(q_in, 16 * n_dma * (h + 1))
                    pe.sem_inc(junk, 1)
                    pe.wait_ge(k_in, 16 * (1 if cmp else n_dma) * (h + 1))
                    pe.sem_inc(junk, 1)
                    for j in range(NP):
                        pe.wait_ge(prep_copied, NP * h + j + 1)
                        pe.sem_inc(junk, 1)
                        if j < preps:
                            x = (qn, kn)[j // 2]
                            for i in range(1 if cmp and j == 2 else 4):
                                n = KW if j >= 2 else 128
                                last = nc.tensor.transpose(PS[0:HD, 3072 + 128 * i:3072 + 128 * i + n], x[0:n, 4 * (j % 2) + i, :], E.ident[0:n, 0:n])
                            last.then_inc(prep_done, 1)
                        else:
                            if j == preps:
                                pe.wait_ge(b_in, 16 * (h + 1))
                                pe.sem_inc(junk, 1)
                            c = 512 * (j - preps) if flips == 2 else 896
                            w = min(512, 1024 - c)
                            nc.tensor.matmul(PS[:, 3072:3072 + w], E.flip[:], raw[:, c:c + w], start=True, stop=True).then_inc(prep_done, 1)
                    pe.wait_ge(prep_copied, NP * h + preps + 1)
                    pe.sem_inc(q_free, 1)

                    def scores(n):
                        pe.wait_ge(s_free, TILES * h + n + 1)
                        pe.sem_inc(junk, 1)
                        k = first(n) * 128
                        L = KW if cmp else (n + 1) * 128 - k
                        for a in range(0, L, 512):
                            b = min(L, a + 512)
                            kk = 0 if cmp else k
                            last = nc.tensor.matmul(s_at(n, a, b), qT[:, n * 128:n * 128 + 128], kT[:, kk + a:kk + b], start=True, stop=True)
                        last.then_inc(score, 1)

                    def turn(n):
                        pe.wait_ge(prob, TILES * h + n + 1)
                        pe.sem_inc(junk, 1)
                        for q in range(groups[n]):
                            i = g_before[n] + q
                            pe.wait_ge(turned_copied, NG * h + i + 1)
                            pe.sem_inc(junk, 1)
                            for j in range(4 * q, min(4 * q + 4, count[n])):
                                last = nc.tensor.transpose(t_at(i, 128 * (j % 4), 128 * (j % 4) + 128), S[:, n % 2, j * KW:j * KW + KW], E.ident[:])
                            last.then_inc(turned, 1)

                    def values(n):
                        pe.wait_ge(turned_copied, NG * h + g_before[n + 1] + 2)
                        pe.sem_inc(junk, 1)
                        pe.wait_ge(out_done, TILES * h + n + 1)
                        pe.sem_inc(junk, 1)
                        if n == 0:
                            pe.wait_ge(v_copied, h + 1)
                            pe.sem_inc(junk, 1)
                        for j in range(count[n]):
                            last = nc.tensor.matmul(PS[:, 3584 + (n % 8) * HD:3648 + (n % 8) * HD], pT[0:KW, n % 2, j * 128:j * 128 + 128],
                                                    vs[0:KW, 0 if cmp else first(n) + j, :], start=(j == 0), stop=(j == count[n] - 1))
                        last.then_inc(value, 1)

                    scores(0)
                    scores(1)
                    for n in range(TILES):
                        turn(n)
                        if n + 2 < TILES:
                            scores(n + 2)
                        values(n)

            @block.vector
            def _(dve):
                dve.sem_inc(s_free, 2)
                dve.sem_inc(out_done, 1)
                dve.sem_inc(turned, 1)
                with dve.Fori(0, H) as h:
                    def limits(n):
                        L = KW if cmp else 128 * count[n]
                        dve.wait_ge(score, TILES * h + n + 1)
                        dve.sem_inc(junk, 1)
                        dve.wait_ge(turned, NG * h + (g_before[n - 1] if n >= 2 else 0) + 1)
                        dve.sem_inc(junk, 1)
                        x = S[:, n % 2, 0:L]
                        if cmp:
                            nc.vector.tensor_tensor(x, s_at(n, 0, L), tb[:, 56 - 8 * n:56 - 8 * n + KW], ALU.add)
                        elif fox:
                            nc.vector.scalar_tensor_tensor(x, s_at(n, 0, L), cq[:, n:n + 1], tb[:, 0:L], ALU.add, ALU.add)
                            dve.drain()
                            nc.vector.tensor_tensor(x[:, L - 128:L], x[:, L - 128:L], E.causal[:], ALU.add)
                        else:
                            nc.vector.tensor_tensor(x, s_at(n, 0, L), tb[:, 1024 - L:1024], ALU.add)
                        dve.drain().then_inc(s_free, 1)
                        nc.vector.tensor_reduce(o[:, n, HD:HD + 1], x, AX.X, ALU.max)
                        dve.drain()
                        nc.vector.tensor_scalar(st[:, n, 1:2], o[:, n, HD:HD + 1], -1.0, -0.1 * NEG, ALU.mult, ALU.min).then_inc(limit, 1)

                    def finish(n):
                        dve.wait_ge(value, TILES * h + n + 2)
                        dve.sem_inc(junk, 1)
                        nc.vector.tensor_scalar(st[:, n, 2:3], o[:, n, HD + 1:HD + 2], TINY, None, ALU.max)
                        dve.drain()
                        nc.vector.reciprocal(st[:, n, 3:4], st[:, n, 2:3])
                        dve.drain()
                        nc.vector.tensor_scalar(o[:, n, 0:HD], PS[:, 3584 + (n % 8) * HD:3648 + (n % 8) * HD], st[:, n, 3:4], None, ALU.mult).then_inc(out_done, 1)

                    if cmp or fox:
                        dve.wait_ge(b_copied, h + 1)
                        dve.sem_inc(junk, 1)
                    else:
                        dve.wait_ge(prep_copied, NP * (h + 1) + 1)
                        dve.sem_inc(junk, 1)
                    if bias[0] == "halves":
                        nc.vector.tensor_tensor(tb[:, 896:1024], tb[:, 896:1024], E.same_half[:], ALU.add)
                    if fox:
                        nc.vector.tensor_copy(cq[:], E.c_all[:, :, ds(h, 1)].rearrange("p n x -> p (n x)"))
                    dve.drain()
                    dve.wait_ge(o_free, h + 1)
                    dve.sem_inc(junk, 1)
                    limits(0)
                    for n in range(TILES):
                        if n + 1 < TILES:
                            limits(n + 1)
                        finish(n)

            @block.scalar
            def _(act):
                act.sem_inc(prep_copied, 1)
                act.sem_inc(turned_copied, 2)
                with act.Fori(0, H) as h:
                    for j in range(NP):
                        act.wait_ge(prep_done, NP * h + j + 1)
                        if j < preps:
                            w = KW if cmp and j == 2 else 512
                            nc.scalar.activation((qT, kT)[j // 2][:, 512 * (j % 2):512 * (j % 2) + w], PS[0:HD, 3072:3072 + w], ACT.Copy,
                                                 scale=SCALE if j < 2 else 1.0).then_inc(prep_copied, 1)
                        else:
                            c = 512 * (j - preps) if flips == 2 else 896
                            w = min(512, 1024 - c)
                            if j == preps:
                                act.sem_inc(junk, 1)
                                act.wait_ge(s_free, TILES * h + 2)
                                act.sem_inc(junk, 1)
                            nc.scalar.activation(tb[:, c:c + w], PS[:, 3072:3072 + w], ACT.Copy).then_inc(prep_copied, 1)
                    if flips:
                        act.wait_ge(prep_copied, NP * (h + 1) + 1)
                        act.sem_inc(b_free, 1)

                    def probs(n):
                        L = KW if cmp else 128 * count[n]
                        act.wait_ge(limit, TILES * h + n + 1)
                        nc.scalar.activation(S[:, n % 2, 0:L], S[:, n % 2, 0:L], ACT.Exp, bias=st[:, n, 1:2],
                                             accum_out=o[:, n, HD + 1:HD + 2]).then_inc(prob, 1)

                    def copies(n):
                        act.wait_ge(value, TILES * h + (n - 2 if n >= 2 else -1) + 2)
                        act.sem_inc(junk, 1)
                        for q in range(groups[n]):
                            i = g_before[n] + q
                            w = 128 * min(4, count[n] - 4 * q)
                            act.wait_ge(turned, NG * h + i + 2)
                            nc.scalar.activation(pT[0:KW, n % 2, 512 * q:512 * q + w], t_at(i, 0, w), ACT.Copy).then_inc(turned_copied, 1)

                    probs(0)
                    for n in range(TILES):
                        if n + 1 < TILES:
                            probs(n + 1)
                        copies(n)


def compress(nc, E, name, NB, pair_tiles, load, loads, out_k, out_v):
    per = min(8, pair_tiles)
    GR = pair_tiles // per
    NCH = pair_tiles * 16
    NK = NCH - 1
    VT = -(-NCH // 128)
    KR = min(128, NCH)
    EV = 2 * GR
    w = per * 128
    with ExitStack() as s:
        sb = lambda n, sh: s.enter_context(nc.sbuf_tensor(f"{name}_{n}", sh, F32))
        sem = s.enter_context(signals(nc, name))
        PS = E.PS
        pairs = sb("pairs", [128, GR, per, 2, 256])
        xT = sb("xT", [128, 2, 2, 8, NCH])
        w1 = sb("w1", [128, 2, 16, CMP_HID])
        w2 = sb("w2", [CMP_HID, 2, HD])
        pe_rows, pe_T = sb("pe_rows", [32, 128]), sb("pe_T", [128, 32])
        pb, npb = sb("pb", [128, 2]), sb("npb", [128, 2])
        ex, xb = sb("ex", [128, NCH]), sb("xb", [128, NCH])
        hid = sb("hid", [128, 2, 2, NCH])
        res = sb("res", [128, 2, VT, 128])
        (w_in, ready, out_ok, hidden, expd, h_free, silu, made, res_free, stored, junk, setup) = map(sem, (
            "w_in", "ready", "out_ok", "hidden", "expd", "h_free", "silu", "made", "res_free", "stored", "junk", "setup"))
        turned, copied = ([sem(f"{n}{l}") for l in range(2)] for n in ("turned", "copied"))
        p_in = [sem(f"p_in{g}") for g in range(GR)]
        p_free = [sem(f"p_free{g}") for g in range(GR)]

        def loop(eng, body):
            if NB == 1:
                body(0)
            else:
                with eng.Fori(0, NB) as b:
                    body(b)

        def copy_turned(eng, b, e, l):
            kv, gr = e // GR, e % GR
            eng.wait_ge(turned[l], EV * b + e + 1)
            for g in range(2):
                dst = xT[64 * l:64 * l + 64, kv, g, :, gr * per * 16:(gr + 1) * per * 16]
                x = PS[64 * g:64 * g + 64, l * 1024:l * 1024 + w].rearrange("p (n l) -> p l n", l=8)
                last = nc.vector.tensor_copy(dst, x) if l else nc.scalar.activation(dst, x, ACT.Copy)
            last.then_inc(copied[l], 1)

        with nc.Block() as block:
            @block.sync
            def _(sp):
                sp.dma_start(w1[:], E.cmp_w1[0].rearrange("k (c p) h -> p k c h", p=128)).then_inc(w_in, 16)
                sp.dma_start(w2[:], E.cmp_w2[0].rearrange("k h d -> h k d")).then_inc(w_in, 16)
                sp.dma_start(pe_rows[:], E.cmp_pe[0].rearrange("k (c l) d -> (k c) (l d)", l=2)).then_inc(w_in, 16)

                def body(b):
                    for g in range(GR):
                        sp.wait_ge(p_free[g], b + 1)
                        sp.sem_inc(junk, 1)
                        load(sp, b, g, pairs[:, g], p_in[g])
                loop(sp, body)

            @block.gpsimd
            def _(pool):
                def body(b):
                    pool.wait_ge(made, 2 * (b + 1))
                    pool.sem_inc(junk, 1)
                    for kv, out in enumerate((out_k, out_v)):
                        o = out(b).rearrange("(i p) w -> p i w", p=KR)
                        pool.dma_start(o, res[0:KR, kv]).then_inc(stored, 16)
                    pool.wait_ge(stored, 32 * (b + 1))
                    pool.sem_inc(res_free, 1)
                loop(pool, body)

            @block.tensor
            def _(pe):
                pe.wait_ge(w_in, 48)
                nc.tensor.transpose(PS[:, 0:32], pe_rows[:], E.ident[0:32, 0:32]).then_inc(setup, 1)
                pe.wait_ge(ready, 1)
                for kv in range(2):
                    for c in range(16):
                        last = nc.tensor.matmul(PS[:, 512 * (kv + 1):512 * (kv + 1) + 1], w1[:, kv, c, :],
                                                pe_T[:, kv * 16 + c:kv * 16 + c + 1], start=(c == 0), stop=(c == 15))
                last.then_inc(setup, 1)
                pe.wait_ge(ready, 2)

                def body(b):
                    for kv in range(2):
                        for gr in range(GR):
                            if kv == 0:
                                pe.wait_ge(p_in[gr], 16 * loads * (b + 1))
                                pe.sem_inc(junk, 1)
                            for l in range(2):
                                pe.wait_ge(copied[l], EV * b + kv * GR + gr + 1)
                                pe.sem_inc(junk, 1)
                                for i in range(per):
                                    last = nc.tensor.transpose(PS[:, l * 1024 + i * 128:l * 1024 + i * 128 + 128],
                                                               pairs[:, gr, i, l, kv * 128:kv * 128 + 128], E.ident[:])
                                last.then_inc(turned[l], 1)
                            if kv:
                                pe.drain().then_inc(p_free[gr], 1)

                    def hidden_layer(kv, g):
                        for l in range(2):
                            pe.wait_ge(copied[l], EV * b + (kv + 1) * GR + 1)
                            pe.sem_inc(junk, 1)
                        pe.wait_ge(h_free, 4 * b + 2 * kv + g + 1)
                        pe.sem_inc(junk, 1)
                        for c in range(16):
                            last = nc.tensor.matmul(PS[:, 2048 + 512 * g:2048 + 512 * g + NK], w1[:, kv, c, :],
                                                    xT[:, kv, g, c % 8, c // 8:c // 8 + NK], start=(c == 0), stop=(c == 15))
                        last.then_inc(hidden, 1)

                    def out_layer(kv):
                        pe.wait_ge(silu, 4 * b + 2 * kv + 3)
                        pe.sem_inc(junk, 1)
                        for i in range(VT):
                            for g in range(2):
                                o = 3072 + 512 * kv + i * 128 + g * 64
                                last = nc.tensor.matmul(PS[0:KR, o:o + 64], hid[:, kv, g, i * 128:i * 128 + KR], w2[:, kv, :], start=True, stop=True)
                        last.then_inc(out_ok, 1)
                    hidden_layer(0, 0)
                    hidden_layer(0, 1)
                    hidden_layer(1, 0)
                    out_layer(0)
                    hidden_layer(1, 1)
                    out_layer(1)
                loop(pe, body)

            @block.vector
            def _(dve):
                dve.sem_inc(h_free, 2)
                dve.sem_inc(silu, 1)
                dve.sem_inc(copied[1], 1)
                nc.vector.memset(hid[:], 0.0)
                dve.wait_ge(setup, 1)
                nc.vector.tensor_copy(pe_T[:], PS[:, 0:32]).then_inc(ready, 1)
                dve.wait_ge(setup, 2)
                for kv in range(2):
                    nc.vector.tensor_copy(pb[:, kv:kv + 1], PS[:, 512 * (kv + 1):512 * (kv + 1) + 1])
                dve.drain()
                nc.vector.tensor_scalar(npb[:], pb[:], -1.0, None, ALU.mult).then_inc(ready, 1)

                def body(b):
                    for e in range(EV):
                        copy_turned(dve, b, e, 1)
                    for k in range(4):
                        kv, g = k // 2, k % 2
                        dve.wait_ge(expd, 4 * b + k + 1)
                        nc.vector.tensor_scalar(xb[:, 0:NK], PS[:, 2048 + 512 * g:2048 + 512 * g + NK], pb[:, kv:kv + 1], None, ALU.add)
                        dve.drain().then_inc(h_free, 1)
                        nc.vector.tensor_scalar(ex[:, 0:NK], ex[:, 0:NK], 1.0, None, ALU.add)
                        dve.drain()
                        nc.vector.reciprocal(ex[:, 0:NK], ex[:, 0:NK])
                        dve.drain()
                        nc.vector.tensor_tensor(hid[:, kv, g, 0:NK], xb[:, 0:NK], ex[:, 0:NK], ALU.mult).then_inc(silu, 1)
                        if k == 2:
                            out_copy(b, 0)
                    out_copy(b, 1)

                def out_copy(b, kv):
                    if kv == 0:
                        dve.wait_ge(res_free, b + 1)
                        dve.sem_inc(junk, 1)
                    dve.wait_ge(out_ok, 2 * b + kv + 1)
                    dve.sem_inc(junk, 1)
                    nc.vector.tensor_copy(res[0:KR, kv].rearrange("p i w -> p (i w)"), PS[0:KR, 3072 + 512 * kv:3072 + 512 * kv + VT * 128]).then_inc(made, 1)
                dve.sem_inc(res_free, 1)
                loop(dve, body)

            @block.scalar
            def _(act):
                act.sem_inc(copied[0], 1)
                for g in range(GR):
                    act.sem_inc(p_free[g], 1)
                act.wait_ge(ready, 2)

                def body(b):
                    for e in range(EV):
                        copy_turned(act, b, e, 0)
                    for k in range(4):
                        kv, g = k // 2, k % 2
                        act.wait_ge(hidden, 4 * b + k + 1)
                        act.sem_inc(junk, 1)
                        act.wait_ge(silu, 4 * b + k + 1)
                        act.sem_inc(junk, 1)
                        nc.scalar.activation(ex[:, 0:NK], PS[:, 2048 + 512 * g:2048 + 512 * g + NK], ACT.Exp,
                                             bias=npb[:, kv:kv + 1], scale=-1.0).then_inc(expd, 1)
                loop(act, body)


def sample_attention(nc, E, name, src, q0, P, R, new_kv, NG, halves, load_k, load_v, loads, bias, out, select=None, rank=False):
    fox = bias[0] == "fox"
    C = 8 * R
    CT = P * C
    W = P * 128
    GT = sum(halves)
    new = new_kv is not None
    NT = new + NG * GT
    NH = len(halves)
    H = 2 * P * R
    with ExitStack() as s:
        sb = lambda n, sh: s.enter_context(nc.sbuf_tensor(f"{name}_{n}", sh, F32))
        sem = s.enter_context(signals(nc, name))
        PS = E.PS
        q_rows = sb("q_rows", [N_TOK, H * HD])
        q_pairs = sb("q_pairs", [N_TOK, P, R, 2 * HD])
        q = sb("q", [128, P, DEC_BATCH, C])
        kb = [sb(f"kb{j}", [128, halves[j], W]) for j in range(NH)]
        vb = [sb(f"vb{j}", [128, halves[j], W]) for j in range(NH)]
        kT = [sb(f"kT{j}", [128, P, halves[j], 128]) for j in range(NH)]
        k_new, v_new = sb("k_new", [128, 1, W]), sb("v_new", [128, 1, W])
        S = sb("S", [128, NT, CT])
        mx, dsum, diag = sb("mx", [128, CT]), sb("dsum", [128, CT]), sb("diag", [CT, CT])
        m, rd = sb("m", [CT, 4]), sb("rd", [CT, 4])
        o_T, o = sb("o_T", [128, CT]), sb("o", [CT, OW])
        if fox:
            decay = sb("decay", [128, C_HEADS, N_PAGES])
            b_new = sb("b_new", [128, CT])
        else:
            step = 13 if NT == 65 else NT
            oh = sb("oh", [33, step, 4, 128])
            bt = sb("bt", [128, NT, CT])
        if select is not None:
            sm = sb("sm", [2, 8, N_PAGES])
        if rank:
            pg = sb("pg", [128, NT, 8])
            pn = sb("pn", [128, NT, CT])
            r_all = sb("r_all", [128, CT])
            blocks = sb("blocks", [128, 4, 129])
            forced = sb("forced", [8, 2, 129])
            imp, top = sb("imp", [8, 129]), sb("top", [8, 8])
            mask = sb("mask", [8, 2, N_PAGES])
        (q_in, q_paired, q_turned, q_copied, zeroed, oh_in, oh_free, bias_mm, bias_ok, b_in, b_free, new_in, new_free, v_new_in, v_new_free,
         mx_ok, mx_T, diag_ok, m_all, shifted, expd, sums, den, o_ok, oT_ok, oT_in, o_done, stored, step_ok, sel_in, sel_mm, sel_free,
         pn_ok, ranked, sel_out, junk) = map(sem, (
             "q_in", "q_paired", "q_turned", "q_copied", "zeroed", "oh_in", "oh_free", "bias_mm", "bias_ok", "b_in", "b_free", "new_in",
             "new_free", "v_new_in", "v_new_free", "mx_ok", "mx_T", "diag_ok", "m_all", "shifted", "expd", "sums", "den", "o_ok",
             "oT_ok", "oT_in", "o_done", "stored", "step_ok", "sel_in", "sel_mm", "sel_free", "pn_ok", "ranked", "sel_out", "junk"))
        k_in, k_free, v_in, v_free, k_turned, k_copied, scored, s_free = (
            [sem(f"{n}{j}") for j in range(NH)] for n in
            ("k_in", "k_free", "v_in", "v_free", "k_turned", "k_copied", "scored", "s_free"))
        uses = [NG + (new and j == 0) for j in range(NH)]

        def groups(eng, body, peel=False):
            if NG == 1:
                body(0, True)
            elif peel:
                with eng.Fori(0, NG - 1) as g:
                    body(g, False)
                body(NG - 1, True)
            else:
                with eng.Fori(0, NG) as g:
                    body(g, False)

        def kt_bank(j):
            return j * 1024

        def sc_bank(j):
            return 2048 + j * 512
        MISC, MISC2, OB = 2048, 2560, 3072

        with nc.Block() as block:
            @block.sync
            def _(sp):
                sp.dma_start(q_rows[:], src[SEQ:N_ALL, q0:q0 + H * HD]).then_inc(q_in, 16)
                if not fox:
                    for c in range(NT // step):
                        if c:
                            sp.wait_ge(oh_free, c)
                        sp.dma_start(oh[:], bias[1][:, c * step:(c + 1) * step]).then_inc(oh_in, 16)
                if rank:
                    sp.dma_start(blocks[:], E.c_blocks).then_inc(sel_in, 16)
                    sp.dma_start(forced[:], E.c_forced).then_inc(sel_in, 16)
                    sp.wait_ge(sel_in, 32)

            @block.gpsimd
            def _(pool):
                nc.gpsimd.memset(q[:], 0.0).then_inc(zeroed, 1)
                nc.gpsimd.memset(k_new[:], 0.0)
                nc.gpsimd.memset(v_new[:], 0.0)
                if fox:
                    nc.gpsimd.memset(b_new[:], NEG)

            @block.tensor
            def _(pe):
                pe.wait_ge(q_paired, 1)
                for p in range(P):
                    for r in range(R):
                        k = p * R + r
                        last = nc.tensor.transpose(PS[:, 32 * k:32 * k + 32], q_pairs[:, p, r, :], E.ident[0:32, 0:32])
                last.then_inc(q_turned, 1)
                if not fox:
                    for c in range(NT // step):
                        pe.wait_ge(oh_in, 16 * (c + 1))
                        if c:
                            pe.wait_ge(bias_ok, c)
                        for i in range(step):
                            for t in range(4):
                                last = nc.tensor.matmul(PS[:, 1024 + (i * 4 + t) * H:1024 + (i * 4 + t + 1) * H], oh[:, i, t, :],
                                                        E.tabx[:, bias[2]:bias[2] + H], start=True, stop=True)
                        last.then_inc(bias_mm, 1)

            @block.vector
            def _(dve):
                dve.wait_ge(q_in, 16)
                for p in range(P):
                    for g in range(2):
                        h0 = (2 * p + g) * R * HD
                        last = nc.vector.tensor_copy(q_pairs[:, p, :, g * HD:(g + 1) * HD], q_rows[:, h0:h0 + R * HD].rearrange("t (r d) -> t r d", r=R))
                last.then_inc(q_paired, 1)
                dve.wait_ge(q_turned, 1)
                dve.wait_ge(zeroed, 1)
                for p in range(P):
                    for r in range(R):
                        k = p * R + r
                        for g in range(2):
                            nc.vector.tensor_scalar(
                                q[64 * g:64 * g + 64, p].rearrange("d b (g r t) -> d g r b t", g=2, r=R)[:, g, r],
                                PS[64 * g:64 * g + 64, 32 * k:32 * k + 32].rearrange("d (b t) -> d b t", t=4), SCALE, None, ALU.mult)
                if not fox:
                    for c in range(NT // step):
                        dve.wait_ge(bias_mm, c + 1)
                        last = nc.vector.tensor_copy(bt[:, c * step:(c + 1) * step, :].rearrange("p i (h t) -> p i t h", t=4),
                                                     PS[:, 1024:1024 + step * 4 * H].rearrange("p (i t h) -> p i t h", t=4, h=H))
                        last.then_inc(bias_ok, 1)

            @block.scalar
            def _(act):
                if not fox and NT // step > 1:
                    for c in range(NT // step - 1):
                        act.wait_ge(bias_mm, c + 1)
                        act.sem_inc(oh_free, 1)

        with nc.Block() as block:
            @block.sync
            def _(sp):
                with sp.Fori(0, DEC_BATCH) as b:
                    if fox:
                        sp.wait_ge(b_free, b + 1)
                        sp.dma_start(decay[:], E.decay[b].rearrange("p (h n) -> p h n", h=C_HEADS)).then_inc(b_in, 16)
                        sp.dma_start(b_new[0:4, :], E.new_bias[ds(b * 4, 4), :]).then_inc(b_in, 16)
                    if select is not None:
                        sp.wait_ge(sel_free, b + 1)
                        sp.dma_start(sm[:], select[b].rearrange("g x n -> x g n")).then_inc(sel_in, 16)
                    if new:
                        sp.wait_ge(new_free, b + 1)
                        sp.dma_start(k_new[0:4, 0, :], src[ds(SEQ + b * 4, 4), new_kv[0]:new_kv[0] + W]).then_inc(new_in, 16)

                    def body(g, last):
                        for j in range(NH):
                            sp.wait_ge(k_free[j], b * NG + g + 1)
                            sp.sem_inc(junk, 1)
                            load_k(sp, b, g, j, kb[j], k_in[j])
                    groups(sp, body)

            @block.gpsimd
            def _(pool):
                with pool.Fori(0, DEC_BATCH) as b:
                    if new:
                        pool.wait_ge(v_new_free, b + 1)
                        pool.sem_inc(junk, 1)
                        pool.dma_start(v_new[0:4, 0, :], src[ds(SEQ + b * 4, 4), new_kv[1]:new_kv[1] + W]).then_inc(v_new_in, 16)

                    def body(g, last):
                        for j in range(NH):
                            pool.wait_ge(v_free[j], b * NG + g + 1)
                            pool.sem_inc(junk, 1)
                            load_v(pool, b, g, j, vb[j], v_in[j])
                    groups(pool, body)

            @block.tensor
            def _(pe):
                def hold(signal, value):
                    pe.wait_ge(signal, value)
                    pe.sem_inc(junk, 1)

                pe.sem_inc(new_free, 1)
                pe.sem_inc(v_new_free, 1)
                if not rank:
                    pe.sem_inc(sel_free, 1)
                for j in range(NH):
                    pe.sem_inc(k_free[j], 1)
                    pe.sem_inc(v_free[j], 1)
                with pe.Fori(0, DEC_BATCH) as b:
                    def turn(j, buf, n):
                        for i in range(n):
                            for p in range(P):
                                last = nc.tensor.transpose(PS[:, kt_bank(j) + (p * n + i) * 128:kt_bank(j) + (p * n + i) * 128 + 128],
                                                           buf[:, i, p * 128:p * 128 + 128], E.ident[:])
                        last.then_inc(k_turned[j], 1)

                    def score(j, n, use):
                        hold(k_copied[j], use + 1)
                        hold(s_free[j], use + 1)
                        for i in range(n):
                            for p in range(P):
                                last = nc.tensor.matmul(PS[:, sc_bank(j) + i * CT + p * C:sc_bank(j) + i * CT + p * C + C],
                                                        kT[j][:, p, i, :], q[:, p, ds(b, 1), :].rearrange("d x c -> d (x c)"), start=True, stop=True)
                        last.then_inc(scored[j], 1)

                    hold(o_done, b + 1)
                    if new:
                        hold(new_in, 16 * (b + 1))
                        turn(0, k_new, 1)
                        pe.drain().then_inc(new_free, 1)
                        score(0, 1, b * uses[0])

                    def body(g, last):
                        for j in range(NH):
                            hold(k_in[j], 16 * loads[j] * (b * NG + g + 1))
                            turn(j, kb[j], halves[j])
                            pe.drain().then_inc(k_free[j], 1)
                        for j in range(NH):
                            score(j, halves[j], b * uses[j] + (new and j == 0) + g)
                    groups(pe, body)
                    if select is not None:
                        hold(sel_in, 16 * (b + 1))
                        for c in range(4):
                            rhs = sm[:, :, 16 * c:16 * c + 16].rearrange("x (g t) n -> x n g t", g=2)
                            for r in range(4):
                                o_ = PS[:, 512 * c:512 * c + 512].rearrange("p (n g r t) -> p n g r t", n=16, g=2, r=4)[:, :, :, r, :]
                                last = nc.tensor.matmul(o_, E.halves[:], rhs, start=True, stop=True)
                        last.then_inc(sel_mm, 1)
                        pe.drain().then_inc(sel_free, 1)
                    hold(mx_ok, b + 1)
                    nc.tensor.transpose(PS[0:CT, MISC:MISC + 128], mx[:], E.ident[:]).then_inc(mx_T, 1)
                    hold(diag_ok, b + 1)
                    nc.tensor.matmul(PS[:, MISC2:MISC2 + CT], E.ones[0:CT, :], diag[:], start=True, stop=True).then_inc(m_all, 1)
                    hold(sums, b + 1)
                    if rank:
                        nc.tensor.matmul(PS[:, MISC:MISC + CT], E.ones[:], dsum[:], start=True, stop=True).then_inc(den, 1)
                        hold(pn_ok, b + 1)
                        for i in range(NT):
                            last = nc.tensor.matmul(PS[0:8, MISC2:MISC2 + 129], pg[:, i, :], blocks[:, i, :], start=(i == 0), stop=(i == NT - 1))
                        last.then_inc(sel_mm, 1)
                        P_ = pn
                    else:
                        nc.tensor.matmul(PS[0:CT, MISC:MISC + 1], dsum[:], E.ones[:, 0:1], start=True, stop=True).then_inc(den, 1)
                        P_ = S

                    def value(buf, n, tile, first, last_):
                        for i in range(n):
                            for p in range(P):
                                x = P_[:, ds(tile + i, 1), p * C:p * C + C].rearrange("k x c -> k (x c)")
                                last = nc.tensor.matmul(PS[:, OB + 512 * p:OB + 512 * p + C], buf[:, i, p * 128:p * 128 + 128], x,
                                                        start=first and i == 0, stop=last_ and i == n - 1)
                        return last
                    if new:
                        hold(v_new_in, 16 * (b + 1))
                        value(v_new, 1, 0, True, False)
                        pe.drain().then_inc(v_new_free, 1)

                    def body(g, last):
                        for j in range(NH):
                            hold(v_in[j], 16 * loads[j] * (b * NG + g + 1))
                            value(vb[j], halves[j], new + g * GT + sum(halves[:j]), not new and j == 0, last and j == NH - 1)
                            pe.drain().then_inc(v_free[j], 1)
                    groups(pe, body, True)
                    pe.drain().then_inc(o_ok, 1)
                    hold(oT_in, b + 1)
                    nc.tensor.transpose(PS[0:CT, MISC:MISC + 128], o_T[:], E.ident[:]).then_inc(oT_ok, 1)

            @block.vector
            def _(dve):
                def hold(signal, value):
                    dve.wait_ge(signal, value)
                    dve.sem_inc(junk, 1)

                dve.sem_inc(o_done, 1)
                dve.sem_inc(b_free, 1)
                for j in range(NH):
                    dve.sem_inc(s_free[j], 1)
                with dve.Fori(0, DEC_BATCH) as b:
                    def take(j, n, tile, use):
                        hold(scored[j], use + 1)
                        x = PS[:, sc_bank(j):sc_bank(j) + n * CT].rearrange("p (i c) -> p i c", c=CT)
                        nc.vector.tensor_tensor(S[:, ds(tile, n), :], x, bt[:, ds(tile, n), :], ALU.add)
                        dve.drain().then_inc(s_free[j], 1)

                    def take_fox(j, n, page, use):
                        hold(scored[j], use + 1)
                        x = PS[:, sc_bank(j):sc_bank(j) + n * CT].rearrange("p (i h t) -> p i h t", h=C_HEADS, t=4)
                        d = decay[:, :, ds(page, n)].rearrange("p h n -> p n h").unsqueeze(3).to_broadcast([128, n, C_HEADS, 4])
                        nc.vector.tensor_tensor(S[:, ds(page + 1, n), :].rearrange("p i (h t) -> p i h t", t=4), x, d, ALU.add)
                        dve.drain().then_inc(s_free[j], 1)
                    if fox:
                        hold(b_in, 32 * (b + 1))
                        hold(scored[0], b * uses[0] + 1)
                        nc.vector.tensor_tensor(S[:, 0, :], PS[:, sc_bank(0):sc_bank(0) + CT], b_new[:], ALU.add)
                        dve.drain().then_inc(s_free[0], 1)
                    elif new:
                        take(0, 1, 0, b * uses[0])

                    def body(g, last):
                        for j in range(NH):
                            use = b * uses[j] + (new and j == 0) + g
                            tile = g * GT + sum(halves[:j])
                            take_fox(j, halves[j], tile, use) if fox else take(j, halves[j], new + tile, use)
                    groups(dve, body)
                    if fox:
                        dve.drain().then_inc(b_free, 1)
                    if select is not None:
                        hold(sel_mm, b + 1)
                        nc.vector.tensor_tensor(S[:, 1:NT, :].rearrange("p i c -> p (i c)"), S[:, 1:NT, :].rearrange("p i c -> p (i c)"),
                                                PS[:, 0:2048], ALU.add)
                        dve.drain()
                    nc.vector.tensor_reduce(mx[:], S[:].rearrange("p i c -> p c i"), AX.X, ALU.max).then_inc(mx_ok, 1)
                    hold(mx_T, b + 1)
                    nc.vector.tensor_reduce(m[:, 0:1], PS[0:CT, MISC:MISC + 128], AX.X, ALU.max)
                    dve.drain()
                    nc.vector.tensor_scalar(m[:, 1:2], m[:, 0:1], 0.1 * NEG, None, ALU.max)
                    dve.drain()
                    nc.vector.tensor_scalar(diag[:], E.ident[0:CT, 0:CT], m[:, 1:2], None, ALU.mult).then_inc(diag_ok, 1)
                    hold(m_all, b + 1)
                    mb = PS[:, MISC2:MISC2 + CT].unsqueeze(1).to_broadcast([128, NT, CT])
                    nc.vector.tensor_tensor(S[:], S[:], mb, ALU.subtract).then_inc(shifted, 1)
                    hold(expd, b + 1)
                    nc.vector.tensor_reduce(dsum[:], S[:].rearrange("p i c -> p c i"), AX.X, ALU.add).then_inc(sums, 1)
                    hold(den, b + 1)
                    if rank:
                        nc.vector.tensor_scalar(r_all[:], PS[:, MISC:MISC + CT], TINY, None, ALU.max)
                        dve.drain()
                        nc.vector.reciprocal(r_all[:], r_all[:])
                        dve.drain()
                        nc.vector.tensor_tensor(pn[:], S[:], r_all[:].unsqueeze(1).to_broadcast([128, NT, CT]), ALU.mult)
                        dve.drain()
                        for i in range(NT):
                            nc.vector.tensor_reduce(pg[:, i, :].rearrange("p (g t) -> p g t", g=2),
                                                    pn[:, i, :].rearrange("p (g r t) -> p g t r", g=2, r=4), AX.X, ALU.add)
                        dve.drain().then_inc(pn_ok, 1)
                        nc.vector.memset(rd[:, 0:1], 1.0)
                    else:
                        nc.vector.tensor_scalar(o[:, HD + 1:HD + 2], PS[0:CT, MISC:MISC + 1], TINY, None, ALU.max)
                        dve.drain()
                        nc.vector.reciprocal(rd[:, 0:1], o[:, HD + 1:HD + 2])
                    nc.vector.tensor_copy(o[:, HD:HD + 1], m[:, 1:2]) if not rank else nc.vector.memset(o[:, HD:OW], 0.0)
                    dve.drain()
                    e = 0 if R == 4 else 2
                    for x in range(2):
                        nc.vector.tensor_scalar(rd[:, 1 + x:2 + x], E.half_of[0:CT, e + x:e + x + 1], rd[:, 0:1], None, ALU.mult)
                    if rank:
                        hold(sel_mm, b + 1)
                        nc.vector.tensor_tensor(imp[:], PS[0:8, MISC2:MISC2 + 129], forced[:, 0, :], ALU.mult)
                        dve.drain()
                        nc.vector.tensor_tensor(imp[:], imp[:], forced[:, 1, :], ALU.add)
                        for k in range(N_SEL // 8):
                            dve.drain()
                            nc.vector.max(top[:], imp[:])
                            dve.drain()
                            nc.vector.match_replace(imp[:], top[:], imp[:], -5.0)
                        dve.drain()
                        hold(sel_free, b + 1)
                        nc.vector.tensor_scalar(mask[:], imp[:, 0:128].rearrange("p (n x) -> p x n", x=2), 0.0, NEG, ALU.is_ge, ALU.mult)
                        dve.drain().then_inc(ranked, 1)
                    hold(o_ok, b + 1)
                    for p in range(P):
                        nc.vector.tensor_copy(o_T[:, p * C:p * C + C], PS[:, OB + 512 * p:OB + 512 * p + C])
                    dve.drain().then_inc(oT_in, 1)
                    hold(oT_ok, b + 1)
                    nc.vector.tensor_scalar(o[:, 0:HD], PS[0:CT, MISC:MISC + 64], rd[:, 1:2], None, ALU.mult)
                    dve.drain()
                    nc.vector.scalar_tensor_tensor(o[:, 0:HD], PS[0:CT, MISC + 64:MISC + 128], rd[:, 2:3], o[:, 0:HD], ALU.mult, ALU.add).then_inc(step_ok, 1)
                    dve.drain()
                    dve.wait_ge(stored, 16 * (b + 1))
                    dve.sem_inc(o_done, 1)

            @block.scalar
            def _(act):
                act.sem_inc(sel_free, 1) if rank else None
                with act.Fori(0, DEC_BATCH) as b:
                    def copy(j, n, use):
                        act.wait_ge(k_turned[j], use + 1)
                        nc.scalar.activation(kT[j][:, :, 0:n, :],
                                             PS[:, kt_bank(j):kt_bank(j) + P * n * 128].rearrange("d (p i k) -> d p i k", p=P, i=n), ACT.Copy).then_inc(k_copied[j], 1)
                    if new:
                        copy(0, 1, b * uses[0])

                    def body(g, last):
                        for j in range(NH):
                            copy(j, halves[j], b * uses[j] + (new and j == 0) + g)
                    groups(act, body)
                    act.wait_ge(shifted, b + 1)
                    nc.scalar.activation(S[:], S[:], ACT.Exp).then_inc(expd, 1)
                    if rank:
                        act.wait_ge(ranked, b + 1)
                        act.dma_start(E.select[b], mask[:]).then_inc(sel_out, 16)
                        act.wait_ge(sel_out, 16 * (b + 1))
                        act.sem_inc(sel_free, 1)
                    act.wait_ge(step_ok, b + 1)
                    act.dma_start(out[ds(SEQ + b * 4, 4), :].rearrange("t (h w) -> h t w", w=OW), o[:]).then_inc(stored, 16)
                    act.wait_ge(stored, 16 * (b + 1))


def page_loader(E, pool, columns, width, value):
    def load(eng, b, g, half, tile, signal):
        for i in range(4):
            page = eng.value_load(E.page_table[ds(b, 1), ds(g * 8 + half * 4 + i, 1)], min_val=0, max_val=N_POOL - 1)
            eng.dma_start(tile[:, i, :], pool[ds(page, 1), :, columns:columns + width].rearrange("x p w -> (x p) w")).then_inc(signal, 16)
    return load


def run_compress(nc, E):
    pool = E.cache_nsa[0].rearrange("n p x g d -> n p (x g d)")

    def load_pages(eng, b, g, tile, signal):
        for i in range(16):
            page = eng.value_load(E.page_table[ds(b, 1), 16 * g + i:16 * g + i + 1], min_val=0, max_val=N_POOL - 1)
            eng.dma_start(tile[64 * (i % 2):64 * (i % 2) + 64, i // 2],
                          pool[ds(page, 1), :, 0:256].rearrange("x (p l) w -> (x p) l w", l=2)).then_inc(signal, 16)

    def load_prompt(eng, b, g, tile, signal):
        for i in range(4):
            eng.dma_start(tile[:, i], E.HE[256 * i:256 * i + 256, KCMP:KCMP + 256].rearrange("(p l) w -> p l w", l=2)).then_inc(signal, 16)
    compress(nc, E, "cmp_p", 1, 4, load_prompt, 4, lambda b: E.kc_p, lambda b: E.vc_p)
    compress(nc, E, "cmp_s", DEC_BATCH, 32, load_pages, 16, lambda b: E.kc_s[b], lambda b: E.vc_s[b])


def run_sample_even(nc, E):
    def loader(x):
        return lambda eng, b, g, half, tile, signal: eng.dma_start(tile[:], x(b)).then_inc(signal, 16)
    sample_attention(nc, E, "s_cmp", E.HE, QA, 1, 4, None, 1, [4],
                     loader(lambda b: E.kc_s[b].rearrange("(i p) w -> p i w", p=128)),
                     loader(lambda b: E.vc_s[b].rearrange("(i p) w -> p i w", p=128)), [1],
                     ("table", E.c_oh_cmp, 0), E.OA[0], rank=True)
    pool = E.cache_nsa[0].rearrange("n p x g d -> n p (x g d)")
    sample_attention(nc, E, "s_sel", E.HE, QA, 1, 4, (KSEL, VSEL), 8, [4, 4],
                     page_loader(E, pool, 256, 128, 0), page_loader(E, pool, 384, 128, 1), [4, 4],
                     ("table", E.c_oh_sel, 0), E.OA[1], select=E.select)
    cw = E.cache_nsa_win[0].rearrange("b (i p) x g d -> x b p i (g d)", p=128)
    sample_attention(nc, E, "s_win", E.HE, QA, 1, 4, (KWIN, VWIN), 1, [4],
                     loader(lambda b: cw[0][b]), loader(lambda b: cw[1][b]), [1], ("table", E.c_oh_win, 0), E.OA[2])
    for g, (w, dil) in enumerate(DILATIONS):
        c = (E.cache_dil_w128, E.cache_dil_w512, E.cache_dil_w2048)[g][0]
        if dil == 1:
            v = c.rearrange("b (i p) x g d -> x b p i (g d)", p=128)
        else:
            v = c.rearrange("b (p i) x g d -> x b p i (g d)", p=128)[:, :, :, 0:4]
        col = B0 + 768 * g
        sample_attention(nc, E, f"s_b{g}", E.HE, col, 2, 1, (col + 256, col + 512), 1, [1 if dil == 1 else 4],
                         loader(lambda b: v[0][b]), loader(lambda b: v[1][b]), [1],
                         ("table", (E.c_oh_b0, E.c_oh_b1, E.c_oh_b2)[g], 8 + 4 * g), E.OB[g])


def gates(nc, E):
    HPB = 8
    with ExitStack() as s:
        sb = lambda n, sh, d=F32: s.enter_context(nc.sbuf_tensor(f"gates_{n}", sh, d))
        sem = s.enter_context(signals(nc, "gates"))
        PS = E.PS
        NTI = TILES + 1
        f, x, e, lf = (sb(n, [128, NTI, C_HEADS]) for n in ("f", "x", "e", "lf"))
        bf = sb("bf", [128, C_HEADS])
        upto, after, seq_upto = sb("upto", [128, 128]), sb("after", [128, 128]), sb("seq_upto", [N_TOK, N_TOK])
        new_mask, new_bias, c_s = sb("new_mask", [N_TOK, 4]), sb("new_bias", [N_TOK, C_HEADS, 4]), sb("c_s", [N_TOK, C_HEADS])
        neg_c = sb("neg_c", [C_HEADS, SEQ])
        table = sb("table", [N_PAGES, DEC_BATCH], mybir.dt.int32)
        L = sb("L", [N_PAGES, PAGE * C_HEADS])
        LT = sb("LT", [128, C_HEADS * N_PAGES])
        tot, tot_b = sb("tot", [N_PAGES, C_HEADS]), sb("tot_b", [N_PAGES, C_HEADS, 128])
        decay = sb("decay", [128, C_HEADS * N_PAGES])
        (cin, zeroed, absd, exp_ok, one_ok, ln_ok, lf_ok, sums, c_ok, turned, neg_ok, out, l_in, l_free, l_turned, lt_ok, summed,
         d_ok, stored, junk, dma_ok, table_in) = map(sem, (
             "cin", "zeroed", "absd", "exp_ok", "one_ok", "ln_ok", "lf_ok", "sums", "c_ok", "turned", "neg_ok", "out", "l_in", "l_free",
             "l_turned", "lt_ok", "summed", "d_ok", "stored", "junk", "dma_ok", "table_in"))
        flat = lambda ap, spec: ap.rearrange(spec)
        with nc.Block() as block:
            @block.sync
            def _(sp):
                for n in range(TILES):
                    sp.dma_start(f[:, n, :], E.HO[n * 128:n * 128 + 128, FC:ZC]).then_inc(cin, 16)
                sp.wait_ge(zeroed, 1)
                sp.dma_start(f[0:N_TOK, TILES, :], E.HO[SEQ:N_ALL, FC:ZC]).then_inc(cin, 16)
                sp.dma_start(bf[:], E.b_f.to_broadcast([128, C_HEADS])).then_inc(cin, 16)
                for t, c in ((upto, E.c_upto), (after, E.c_after), (seq_upto, E.c_seq_upto), (new_mask, E.c_new_mask)):
                    sp.dma_start(t[:], c).then_inc(cin, 16)
                k = 0
                rows = [(E.o_nsa_prompt, E.o_nsa_sample, E.HE, KCMP, 512, SEQ), (E.o_fox_prompt, E.o_fox_sample, E.HO, KC, 512, SEQ)]
                for op, os_, src, c, w, n in rows:
                    sp.dma_start(op.rearrange("a b t x g d -> (a b t) (x g d)"), src[SEQ - n:SEQ, c:c + w]).then_inc(out, 16)
                    sp.dma_start(os_.rearrange("a b t x g d -> (a b t) (x g d)"), src[SEQ:N_ALL, c:c + w]).then_inc(out, 16)
                    k += 2
                rows = [(E.o_win_prompt, E.o_win_sample, KWIN, 256, WIN), (E.o_dil0_prompt, E.o_dil0_sample, B0 + 256, 512, 128),
                        (E.o_dil1_prompt, E.o_dil1_sample, B0 + 1024, 512, 512), (E.o_dil2_prompt, E.o_dil2_sample, B0 + 1792, 512, SEQ)]
                for op, os_, c, w, n in rows:
                    sp.dma_start(op.rearrange("a b t x g d -> (a b t) (x g d)"), E.HE[SEQ - n:SEQ, c:c + w]).then_inc(out, 16)
                    v = os_.rearrange("a b t x g d -> (a b) t (x g d)")
                    T = v.shape[1]
                    sp.dma_start(v[:, T - DEC_SEQ:T, :], E.HE[SEQ:N_ALL, c:c + w].rearrange("(b t) w -> b t w", t=DEC_SEQ)).then_inc(out, 16)
                    k += 2
                sp.wait_ge(lf_ok, 1)
                sp.dma_start(E.o_logf_prompt[0, 0].rearrange("(n p) h -> p n h", p=128), lf[:, 0:TILES, :]).then_inc(out, 16)
                sp.dma_start(E.o_logf_sample.rearrange("a b t h -> (a b t) h"), lf[0:N_TOK, TILES, :]).then_inc(out, 16)
                sp.wait_ge(neg_ok, 2)
                sp.dma_start(E.neg_c, neg_c[:]).then_inc(out, 16)
                sp.dma_start(E.new_bias, new_bias[:].rearrange("p h t -> p (h t)")).then_inc(out, 16)
                sp.wait_ge(out, 16 * (k + 4))
                with sp.Fori(0, DEC_BATCH) as b:
                    sp.wait_ge(d_ok, b + 1)
                    sp.dma_start(E.decay[b], decay[:]).then_inc(stored, 16)
                    sp.wait_ge(stored, 16 * (b + 1))
                    sp.sem_inc(dma_ok, 1)

            @block.gpsimd
            def _(pool):
                nc.gpsimd.memset(f[:, TILES, :], 0.0).then_inc(zeroed, 1)
                with nc.allow_non_contiguous_dma(reason="the page table turned, 512 words"):
                    pool.dma_start(table[:], E.page_table.rearrange("b n -> n b")).then_inc(table_in, 16)
                pool.wait_ge(table_in, 16)
                for b in range(DEC_BATCH):
                    if b:
                        pool.wait_ge(l_free, b)
                    nc.gpsimd.indirect_dma_start(L[:], None, E.cache_fox_logf[0].rearrange("n p h -> n (p h)"),
                                                 bass.IndirectOffsetOnAxis(table[:, b:b + 1], 0)).then_inc(l_in, 16)

            @block.scalar
            def _(act):
                act.wait_ge(absd, 1)
                nc.scalar.activation(e[:], x[:], ACT.Exp, scale=-1.0).then_inc(exp_ok, 1)
                act.wait_ge(one_ok, 1)
                nc.scalar.activation(e[:], e[:], ACT.Ln).then_inc(ln_ok, 1)

            @block.vector
            def _(dve):
                dve.sem_inc(dma_ok, 1)
                dve.wait_ge(cin, 16 * 14)
                nc.vector.tensor_tensor(f[:], f[:], bf[:].unsqueeze(1).to_broadcast([128, NTI, C_HEADS]), ALU.add)
                dve.drain()
                nc.vector.tensor_scalar(x[:], f[:], -1.0, None, ALU.mult)
                dve.drain()
                nc.vector.tensor_tensor(x[:], x[:], f[:], ALU.max).then_inc(absd, 1)
                dve.wait_ge(exp_ok, 1)
                nc.vector.tensor_scalar(e[:], e[:], 1.0, None, ALU.add).then_inc(one_ok, 1)
                dve.wait_ge(ln_ok, 1)
                nc.vector.scalar_tensor_tensor(lf[:], f[:], 0.0, e[:], ALU.min, ALU.subtract).then_inc(lf_ok, 1)
                dve.wait_ge(sums, 1)
                nc.vector.tensor_copy(E.c_all[:].rearrange("p n h -> p (n h)"), PS[:, 0:128])
                nc.vector.tensor_scalar(c_s[:], PS[0:N_TOK, 128:144], -1.0, None, ALU.mult)
                dve.drain().then_inc(c_ok, 1)
                nc.vector.tensor_tensor(new_bias[:], c_s[:].unsqueeze(2).to_broadcast([N_TOK, C_HEADS, 4]),
                                        new_mask[:].unsqueeze(1).to_broadcast([N_TOK, C_HEADS, 4]), ALU.add).then_inc(neg_ok, 1)
                dve.wait_ge(turned, 1)
                nc.vector.tensor_scalar(neg_c[:], PS[0:C_HEADS, 1024:2048], -1.0, None, ALU.mult).then_inc(neg_ok, 1)
                with dve.Fori(0, DEC_BATCH) as b:
                    dve.wait_ge(l_in, 16 * b + 16)
                    nc.vector.tensor_reduce(tot[:], L[:].rearrange("n (p h) -> n h p", h=C_HEADS), AX.X, ALU.add)
                    dve.drain()
                    nc.vector.tensor_copy(tot_b[:], tot[:].unsqueeze(2).to_broadcast([N_PAGES, C_HEADS, 128]))
                    dve.drain()
                    dve.wait_ge(l_turned, b + 1)
                    nc.vector.tensor_copy(LT[:], PS[:, 2048:3072]).then_inc(lt_ok, 1)
                    dve.wait_ge(summed, b + 1)
                    dve.sem_inc(junk, 1)
                    dve.sem_inc(l_free, 1)
                    dve.wait_ge(dma_ok, b + 1)
                    nc.vector.tensor_copy(decay[:], PS[:, 3072:4096]).then_inc(d_ok, 1)

            @block.tensor
            def _(pe):
                pe.wait_ge(lf_ok, 1)
                for n in range(TILES):
                    nc.tensor.matmul(PS[:, n * 16:n * 16 + 16], upto[:], lf[:, n, :], start=True, stop=(n == 0))
                    for m in range(n):
                        nc.tensor.matmul(PS[:, n * 16:n * 16 + 16], E.ones[:], lf[:, m, :], start=False, stop=(m == n - 1))
                nc.tensor.matmul(PS[0:N_TOK, 128:144], seq_upto[:], lf[0:N_TOK, TILES, :], start=True, stop=True).then_inc(sums, 1)
                pe.wait_ge(c_ok, 1)
                for n in range(TILES):
                    last = nc.tensor.transpose(PS[0:C_HEADS, 1024 + n * 128:1152 + n * 128], E.c_all[:, n, :], E.ident[:])
                last.then_inc(turned, 1)
                with pe.Fori(0, DEC_BATCH) as b:
                    pe.wait_ge(l_in, 16 * b + 16)
                    pe.sem_inc(junk, 1)
                    pe.wait_ge(dma_ok, b + 1)
                    pe.sem_inc(junk, 1)
                    v = L[:].rearrange("n (p h) -> n h p", h=C_HEADS)
                    for h in range(C_HEADS):
                        last = nc.tensor.transpose(PS[:, 2048 + h * 64:2112 + h * 64], v[:, h, :], E.ident[0:N_PAGES, 0:N_PAGES])
                    last.then_inc(l_turned, 1)
                    pe.wait_ge(lt_ok, b + 1)
                    pe.sem_inc(junk, 1)
                    for c in range(2):
                        nc.tensor.matmul(PS[:, 3072 + 512 * c:3584 + 512 * c], after[:], LT[:, 512 * c:512 * c + 512], start=True, stop=False)
                        for h in range(HPB * c, HPB * c + HPB):
                            last = nc.tensor.matmul(PS[:, 3072 + h * 64:3136 + h * 64], tot_b[:, h, :], after[0:N_PAGES, 0:N_PAGES],
                                                    start=False, stop=(h % HPB == HPB - 1))
                    last.then_inc(summed, 1)


def mix(nc, E, name, even, weights, x_of, out_of, gain):
    KT = weights.shape[0] // 128
    WZ = KT * 128
    with ExitStack() as s:
        sb = lambda n, sh: s.enter_context(nc.sbuf_tensor(f"{name}_{n}", sh, F32))
        sem = s.enter_context(signals(nc, name))
        PS = E.PS
        w = sb("w", [128, KT, D_MODEL])
        z = sb("z", [128, 2, WZ])
        x = sb("x", [128, 2, D_MODEL])
        if even:
            gt = sb("gt", [128, 2, 24])
            oa, ob = sb("oa", [128, 2, 3, A_HEADS, OW]), sb("ob", [128, 2, 3, B_HEADS, OW])
            eg, ta = sb("eg", [128, 3, A_HEADS]), sb("ta", [128, 3, A_HEADS * HD])
            mm, wt, den, tb = sb("mm", [128, B_HEADS]), sb("wt", [128, 3, B_HEADS]), sb("den", [128, B_HEADS]), sb("tb", [128, 3, B_HEADS * HD])
        else:
            oc = sb("oc", [128, 2, C_HEADS, OW])
            g = sb("g", [128, D_MODEL])
        ez = sb("ez", [128, WZ])
        mixed, mT = sb("mixed", [128, WZ]), sb("mT", [128, KT, 128])
        y, sq, st = sb("y", [128, D_MODEL]), sb("sq", [128, D_MODEL]), sb("st", [128, 4])
        (w_in, exp_ok, mx_ok, wexp, mixed_ok, turned, mT_ok, prod, y_ok, sumsq, mean, root, stored, junk, ez_free) = map(sem, (
            "w_in", "exp_ok", "mx_ok", "wexp", "mixed_ok", "turned", "mT_ok", "prod", "y_ok", "sumsq", "mean", "root", "stored", "junk", "ez_free"))
        loaded, freed = [sem("loaded0"), sem("loaded1")], [sem("freed0"), sem("freed1")]
        n_in = 9 if even else 3

        def tiles(eng, body):
            with eng.Fori(0, TILES // 2) as i2:
                body(2 * i2, i2, 0, 128)
                body(2 * i2 + 1, i2, 1, 128)
            body(TILES, TILES // 2, 0, N_TOK)

        with nc.Block() as block:
            @block.sync
            def _(sp):
                sp.dma_start(w[:], weights.rearrange("(k p) n -> p k n", p=128)).then_inc(w_in, 16)
                if not even:
                    sp.dma_start(g[:], gain.to_broadcast([128, D_MODEL])).then_inc(w_in, 16)

                def body(i, i2, h, n):
                    rows = ds(i * 128, n)
                    sp.wait_ge(freed[h], i2 + 1)
                    sp.dma_start(x[0:n, h], x_of(i, n)).then_inc(loaded[h], 16)
                    if even:
                        sp.dma_start(gt[0:n, h], E.HE[rows, GA:GA + 24]).then_inc(loaded[h], 16)
                        sp.dma_start(z[0:n, h, 0:512], E.HE[rows, ZA:ZA + 512]).then_inc(loaded[h], 16)
                        sp.dma_start(z[0:n, h, 512:768], E.HE[rows, ZB:ZB + 256]).then_inc(loaded[h], 16)
                        for k in range(3):
                            sp.dma_start(oa[0:n, h, k, :, 0:HD], E.OA[k][rows].rearrange("t (h w) -> t h w", w=OW)[:, :, 0:HD]).then_inc(loaded[h], 16)
                        for k in range(3):
                            sp.dma_start(ob[0:n, h, k].rearrange("t h w -> t (h w)"), E.OB[k][rows]).then_inc(loaded[h], 16) if k < 2 else \
                                sp.dma_start(ob[0:n, h, k].rearrange("t h w -> t (h w)"), E.OB[k][rows]).then_inc(loaded[h], 16)
                    else:
                        sp.dma_start(z[0:n, h], E.HO[rows, ZC:ODD_IN]).then_inc(loaded[h], 16)
                        sp.dma_start(oc[0:n, h].rearrange("t h w -> t (h w)"), E.OC[rows]).then_inc(loaded[h], 16)
                tiles(sp, body)

            @block.scalar
            def _(act):
                def body(i, i2, h, n):
                    act.wait_ge(loaded[h], 16 * (10 if even else 3) * (i2 + 1))
                    act.sem_inc(junk, 1)
                    act.wait_ge(ez_free, i + 1)
                    if even:
                        nc.scalar.activation(eg[0:n].rearrange("p k h -> p (k h)"), gt[0:n, h], ACT.Exp, scale=-1.0)
                    nc.scalar.activation(ez[0:n], z[0:n, h], ACT.Exp, scale=-1.0)
                    act.drain().then_inc(exp_ok, 1)
                    if even:
                        act.wait_ge(mx_ok, i + 1)
                        nc.scalar.activation(wt[0:n], wt[0:n], ACT.Exp).then_inc(wexp, 1)
                    act.wait_ge(turned, i + 1)
                    nc.scalar.activation(mT[:, :, 0:n], PS[:, 0:KT * 128].rearrange("p (k t) -> p k t", k=KT)[:, :, 0:n], ACT.Copy).then_inc(mT_ok, 1)
                    if not even:
                        act.wait_ge(prod, i + 1)
                        act.sem_inc(junk, 1)
                        act.wait_ge(sumsq, 2 * i + 1)
                        nc.scalar.activation(sq[0:n], y[0:n], ACT.Square, accum_out=st[0:n, 0:1]).then_inc(sumsq, 1)
                        act.wait_ge(mean, i + 1)
                        nc.scalar.activation(st[0:n, 2:3], st[0:n, 1:2], ACT.Sqrt).then_inc(root, 1)
                    act.wait_ge(y_ok, i + 1)
                    act.dma_start(out_of(i, n), y[0:n]).then_inc(stored, 16)
                    act.wait_ge(stored, 16 * (i + 1))
                    act.sem_inc(ez_free, 1)
                tiles(act, body)

            @block.vector
            def _(dve):
                V = nc.vector
                dve.sem_inc(ez_free, 1)
                dve.sem_inc(freed[0], 1)
                dve.sem_inc(freed[1], 1)
                dve.wait_ge(w_in, 16 if even else 32)

                def silu(n, h):
                    V.tensor_scalar(ez[0:n], ez[0:n], 1.0, None, ALU.add)
                    dve.drain()
                    V.reciprocal(ez[0:n], ez[0:n])
                    dve.drain()
                    V.tensor_tensor(ez[0:n], ez[0:n], z[0:n, h], ALU.mult)
                    dve.drain()

                def body(i, i2, h, n):
                    dve.wait_ge(exp_ok, i + 1)
                    dve.sem_inc(junk, 1)
                    if even:
                        V.tensor_tensor(mm[0:n], ob[0:n, h, 0, :, HD], ob[0:n, h, 1, :, HD], ALU.max)
                        dve.drain()
                        V.tensor_tensor(mm[0:n], mm[0:n], ob[0:n, h, 2, :, HD], ALU.max)
                        dve.drain()
                        V.tensor_tensor(wt[0:n], ob[0:n, h, :, :, HD], mm[0:n].unsqueeze(1).to_broadcast([n, 3, B_HEADS]), ALU.subtract).then_inc(mx_ok, 1)
                        silu(n, h)
                        V.tensor_scalar(eg[0:n], eg[0:n], 1.0, None, ALU.add)
                        dve.drain()
                        V.reciprocal(eg[0:n], eg[0:n])
                        dve.drain()
                        for k in range(3):
                            V.tensor_tensor(ta[0:n, k].rearrange("p (h d) -> p h d", d=HD), oa[0:n, h, k, :, 0:HD],
                                            eg[0:n, k].unsqueeze(2).to_broadcast([n, A_HEADS, HD]), ALU.mult)
                        dve.drain()
                        V.tensor_tensor(ta[0:n, 0], ta[0:n, 0], ta[0:n, 1], ALU.add)
                        dve.wait_ge(wexp, i + 1)
                        V.tensor_tensor(wt[0:n], wt[0:n], ob[0:n, h, :, :, HD + 1], ALU.mult)
                        dve.drain()
                        V.tensor_tensor(ta[0:n, 0], ta[0:n, 0], ta[0:n, 2], ALU.add)
                        V.tensor_reduce(den[0:n], wt[0:n].rearrange("p k h -> p h k"), AX.X, ALU.add)
                        dve.drain()
                        V.reciprocal(den[0:n], den[0:n])
                        V.tensor_tensor(mixed[0:n, 0:512], ta[0:n, 0], ez[0:n, 0:512], ALU.mult)
                        dve.drain()
                        V.tensor_tensor(wt[0:n], wt[0:n], den[0:n].unsqueeze(1).to_broadcast([n, 3, B_HEADS]), ALU.mult)
                        dve.drain()
                        for k in range(3):
                            V.tensor_tensor(tb[0:n, k].rearrange("p (h d) -> p h d", d=HD), ob[0:n, h, k, :, 0:HD],
                                            wt[0:n, k].unsqueeze(2).to_broadcast([n, B_HEADS, HD]), ALU.mult)
                        dve.drain()
                        V.tensor_tensor(tb[0:n, 0], tb[0:n, 0], tb[0:n, 1], ALU.add)
                        dve.drain()
                        V.tensor_tensor(tb[0:n, 0], tb[0:n, 0], tb[0:n, 2], ALU.add)
                        dve.drain()
                        V.tensor_tensor(mixed[0:n, 512:768], tb[0:n, 0], ez[0:n, 512:768], ALU.mult).then_inc(mixed_ok, 1)
                    else:
                        silu(n, h)
                        V.tensor_tensor(mixed[0:n].rearrange("p (h d) -> p h d", d=HD), oc[0:n, h, :, 0:HD],
                                        ez[0:n].rearrange("p (h d) -> p h d", d=HD), ALU.mult).then_inc(mixed_ok, 1)
                    dve.wait_ge(prod, i + 1)
                    dve.sem_inc(junk, 1)
                    dve.wait_ge(ez_free, i + 1)
                    dve.sem_inc(junk, 1)
                    V.tensor_tensor(y[0:n], PS[0:n, 1024:2048], x[0:n, h], ALU.add)
                    dve.drain().then_inc(freed[h], 1)
                    if even:
                        dve.sem_inc(y_ok, 1)
                    else:
                        dve.sem_inc(sumsq, 1)
                        dve.wait_ge(sumsq, 2 * i + 2)
                        V.tensor_scalar(st[0:n, 1:2], st[0:n, 0:1], 1.0 / D_MODEL, EPS, ALU.mult, ALU.add).then_inc(mean, 1)
                        dve.wait_ge(root, i + 1)
                        V.reciprocal(st[0:n, 3:4], st[0:n, 2:3])
                        dve.drain()
                        V.scalar_tensor_tensor(y[0:n], y[0:n], st[0:n, 3:4], g[0:n], ALU.mult, ALU.mult).then_inc(y_ok, 1)
                tiles(dve, body)

            @block.tensor
            def _(pe):
                def body(i, i2, h, n):
                    pe.wait_ge(mixed_ok, i + 1)
                    pe.sem_inc(junk, 1)
                    for k in range(KT):
                        last = nc.tensor.transpose(PS[:, k * 128:k * 128 + n], mixed[0:n, k * 128:k * 128 + 128], E.ident[0:n, 0:n])
                    last.then_inc(turned, 1)
                    pe.wait_ge(mT_ok, i + 1)
                    pe.sem_inc(junk, 1)
                    for c in range(2):
                        for k in range(KT):
                            last = nc.tensor.matmul(PS[0:n, 1024 + 512 * c:1536 + 512 * c], mT[:, k, 0:n], w[:, k, 512 * c:512 * c + 512],
                                                    start=(k == 0), stop=(k == KT - 1))
                    last.then_inc(prod, 1)
                pe.wait_ge(w_in, 16 if even else 32)
                tiles(pe, body)


def load_constants(nc, E, s):
    sb = lambda n, sh: s.enter_context(nc.sbuf_tensor(n, sh, F32))
    E.PS = s.enter_context(nc.psum_tensor("PS", [128, 4096], F32))
    E.ident, E.flip, E.causal, E.same_half = (sb(n, [128, 128]) for n in ("ident", "flip", "causal", "same_half"))
    E.tabx = sb("tabx", [33, BIAS_HEADS])
    E.ones = sb("ones", [128, 128])
    E.halves = sb("halves", [2, 128])
    E.half_of = sb("half_of", [64, 4])
    E.c_all = sb("c_all", [128, TILES, C_HEADS])
    cin, table = s.enter_context(nc.semaphore("constants_in")), s.enter_context(nc.semaphore("table_in"))
    E.states = s.enter_context(nc.semaphore("states"))
    mask_row = s.enter_context(nc.semaphore("mask_row"))
    with nc.Block() as block:
        @block.sync
        def _(sp):
            for t, c in ((E.ident, E.c_ident), (E.flip, E.c_flip), (E.causal, E.c_causal), (E.same_half, E.c_same_half), (E.half_of, E.c_half_of), (E.halves, E.c_halves)):
                sp.dma_start(t[:], c).then_inc(cin, 16)
            sp.wait_ge(mask_row, 1)
            sp.dma_start(E.tabx[0:32, :], E.rel_bias).then_inc(table, 16)
            sp.wait_ge(cin, 96)
            sp.wait_ge(table, 16)

        @block.gpsimd
        def _(pool):
            nc.gpsimd.memset(E.ones[:], 1.0)
            nc.gpsimd.memset(E.tabx[:], NEG).then_inc(mask_row, 1)


def scratch(nc, E):
    dram = lambda n, sh: nc.dram_tensor(n, sh, F32, kind="Internal").ap()
    E.HE, E.HO = dram("HE", (N_ALL, EVEN_IN)), dram("HO", (N_ALL, ODD_IN))
    E.rows = dram("bias_rows", (29, 1152))
    E.cmp_rows = dram("cmp_rows", (8, 128, 120))
    E.kc_p, E.vc_p = dram("kc_p", (CMP_OUT[1] + 1, 128)), dram("vc_p", (CMP_OUT[1] + 1, 128))
    E.kc_s, E.vc_s = dram("kc_s", (DEC_BATCH, CMP_OUT[0] + 1, 128)), dram("vc_s", (DEC_BATCH, CMP_OUT[0] + 1, 128))
    E.decay = dram("decay", (DEC_BATCH, 128, C_HEADS * N_PAGES))
    E.new_bias = dram("new_bias", (N_TOK, C_HEADS * 4))
    E.neg_c = dram("neg_c", (C_HEADS, SEQ))
    E.OA = [dram(f"OA{i}", (N_ALL, A_HEADS * OW)) for i in range(3)]
    E.OB = [dram(f"OB{i}", (N_ALL, B_HEADS * OW)) for i in range(3)]
    E.OC = dram("OC", (N_ALL, C_HEADS * OW))
    E.select = dram("select", (DEC_BATCH, 8, 2, N_PAGES))
    E.H1 = dram("H1", (N_ALL, D_MODEL))


def program(nc, E):
    with ExitStack() as s:
        scratch(nc, E)
        load_constants(nc, E, s)
        make_bias_rows(nc, E)
        rows = lambda ap: ap.rearrange("a t d -> (a t) d")
        either = lambda p, q: lambda i, n: rows(p)[ds(i * 128, n), :] if n == 128 else rows(q)
        h1 = lambda i, n: E.H1[ds(i * 128, n), :]
        x_in = either(E.x_prompt, E.x_sample)
        project(nc, E, "even", x_in, E.norm_e, E.w_in_e[0], E.HE, 512, 8, 280, shift_states)
        run_compress(nc, E)
        prompt_attention(nc, E, "cmp", A_KV, 4, E.HE, QA, 0, 0, E.OA[0], ("cmp",), lambda n: n)
        prompt_attention(nc, E, "win", A_KV, 4, E.HE, QA, KWIN, VWIN, E.OA[2], ("rows", 0), lambda n: max(0, n - 4))
        prompt_attention(nc, E, "sel", A_KV, 4, E.HE, QA, KSEL, VSEL, E.OA[1], ("rows", 8), lambda n: 0)
        prompt_attention(nc, E, "dil0", B_HEADS, 1, E.HE, B0, B0 + 256, B0 + 512, E.OB[0], ("rows", 16), lambda n: max(0, n - 1))
        prompt_attention(nc, E, "dil1", B_HEADS, 1, E.HE, B0 + 768, B0 + 1024, B0 + 1280, E.OB[1], ("rows", 20), lambda n: n - n % 2, 4)
        prompt_attention(nc, E, "dil2", B_HEADS, 1, E.HE, B0 + 1536, B0 + 1792, B0 + 2048, E.OB[2], ("halves", 24), lambda n: n, 16)
        run_sample_even(nc, E)
        mix(nc, E, "out_e", True, E.w_out_e[0], x_in, h1, None)
        project(nc, E, "odd", h1, E.norm_o, E.w_in_o[0], E.HO, 368, 7, 0)
        gates(nc, E)
        prompt_attention(nc, E, "fox", C_KV, 4, E.HO, QC, KC, VC, E.OC, ("fox",), lambda n: 0)
        pool = E.cache_fox[0].rearrange("n p x g d -> n p (x g d)")
        sample_attention(nc, E, "s_fox", E.HO, QC, 2, 4, (KC, VC), 8, [4, 4], page_loader(E, pool, 0, 256, 0),
                         page_loader(E, pool, 256, 256, 1), [4, 4], ("fox",), E.OC)
        mix(nc, E, "out_o", False, E.w_out_o[0], h1, either(E.o_y_prompt, E.o_y_sample), E.norm_f.unsqueeze(0))
        with nc.Block() as block:
            @block.sync
            def _(sp):
                sp.wait_ge(E.states, 16 * 4 * DEC_BATCH)


_INS = ["x_prompt", "x_sample", "cache_nsa", "cache_nsa_win", "cache_dil_w128", "cache_dil_w512", "cache_dil_w2048",
        "cache_fox", "cache_fox_logf", "page_table", "rel_bias", "norm_e", "w_in_e", "cmp_pe", "cmp_w1", "cmp_w2",
        "w_out_e", "norm_o", "w_in_o", "b_f", "w_out_o", "norm_f"]
_OUTS = [
    ("y_prompt", (1, SEQ, D_MODEL)), ("y_sample", (DEC_BATCH, DEC_SEQ, D_MODEL)),
    ("nsa_prompt", (1, 1, SEQ, 4, A_KV, HD)), ("nsa_sample", (1, DEC_BATCH, DEC_SEQ, 4, A_KV, HD)),
    ("win_prompt", (1, 1, WIN, 2, A_KV, HD)), ("win_sample", (1, DEC_BATCH, WIN, 2, A_KV, HD)),
    ("dil0_prompt", (1, 1, 128, 2, B_HEADS, HD)), ("dil0_sample", (1, DEC_BATCH, 128, 2, B_HEADS, HD)),
    ("dil1_prompt", (1, 1, 512, 2, B_HEADS, HD)), ("dil1_sample", (1, DEC_BATCH, 512, 2, B_HEADS, HD)),
    ("dil2_prompt", (1, 1, SEQ, 2, B_HEADS, HD)), ("dil2_sample", (1, DEC_BATCH, 2048, 2, B_HEADS, HD)),
    ("fox_prompt", (1, 1, SEQ, 2, C_KV, HD)), ("fox_sample", (1, DEC_BATCH, DEC_SEQ, 2, C_KV, HD)),
    ("logf_prompt", (1, 1, SEQ, C_HEADS)), ("logf_sample", (1, DEC_BATCH, DEC_SEQ, C_HEADS)),
]


def kernel(**inputs):
    import concourse.bacc as _bacc
    from concourse.bass_utils import run_bass_kernel_spmd as _run

    nc = _bacc.Bacc("TRN2", target_bir_lowering=False, num_devices=1)
    E, arrays = Env(), {}
    for name in _INS:
        a = np.ascontiguousarray(inputs[name])
        arrays[f"in_{name}"] = a
        E.__dict__[name] = nc.dram_tensor(f"in_{name}", a.shape, mybir.dt.from_np(a.dtype), kind="ExternalInput").ap()
    for name, a in constants().items():
        a = np.ascontiguousarray(a)
        arrays[f"const_{name}"] = a
        E.__dict__["c_" + name] = nc.dram_tensor(f"const_{name}", a.shape, F32, kind="ExternalInput").ap()
    for name, shape in _OUTS:
        E.__dict__["o_" + name] = nc.dram_tensor(f"out_{name}", shape, F32, kind="ExternalOutput").ap()
    program(nc, E)
    r = _run(nc, [arrays], core_ids=[0])
    return tuple(r.results[0][f"out_{name}"] for name, _ in _OUTS)
```
